# Optimizing a Trainium2 kernel written in Bass

```python
import jax, jax.numpy as jnp
from jax import lax
import numpy as np

D_MODEL = 1024
BATCH = 1
SEQ = 1024
DEPTH = 1

MEM_LEN = 256
MIX_WIDTH = D_MODEL
FOX_HEADS = 8
FOX_HEAD_DIM = (MIX_WIDTH // 2) // FOX_HEADS
FOX_WIDTH = FOX_HEADS * FOX_HEAD_DIM
GDN_HEADS = 4
GDN_HEAD_DIM = (MIX_WIDTH // 2) // GDN_HEADS
GDN_WIDTH = GDN_HEADS * GDN_HEAD_DIM
CONV_WIDTH = 4
GDN_CHUNK = 64
Q_BLOCK = 128
XATTN_HEADS = 4
XATTN_HEAD_DIM = 128
XATTN_WIDTH = XATTN_HEADS * XATTN_HEAD_DIM
D_FF = 4 * D_MODEL
EPS = 1e-6
NEG_INF = -1e30

IN_SIZES = [3 * FOX_WIDTH, FOX_HEADS, 3 * GDN_WIDTH, GDN_HEADS, GDN_HEADS, GDN_WIDTH]
IN_DIM = sum(IN_SIZES)
IN_OFFSETS = [int(o) for o in np.cumsum(IN_SIZES)[:-1]]

kernel_name = "hymba_fox_gdn_memxattn_block"

def rms_norm(x, g):
    xf = x.astype(jnp.float32)
    y = xf * lax.rsqrt(jnp.mean(xf * xf, axis=-1, keepdims=True) + EPS)
    return (y * g.astype(jnp.float32)).astype(x.dtype)

def l2_norm(x):
    xf = x.astype(jnp.float32)
    return (xf * lax.rsqrt(jnp.sum(xf * xf, axis=-1, keepdims=True) + EPS)).astype(x.dtype)

def causal_depthwise_conv(x, w):
    C = x.shape[-1]
    return lax.conv_general_dilated(
        x, w[:, None, :].astype(x.dtype), window_strides=(1,),
        padding=((CONV_WIDTH - 1, 0),),
        dimension_numbers=("NWC", "WIO", "NWC"),
        feature_group_count=C)

def forgetting_attention(q, k, v, f_logit):
    B, S, H, Dh = q.shape
    nb = S // Q_BLOCK
    scale = Dh ** -0.5
    c = jnp.cumsum(jax.nn.log_sigmoid(f_logit.astype(jnp.float32)), axis=1)
    c = c.transpose(0, 2, 1)
    q_blocks = q.reshape(B, nb, Q_BLOCK, H, Dh).transpose(1, 0, 3, 2, 4)
    c_blocks = c.reshape(B, H, nb, Q_BLOCK).transpose(2, 0, 1, 3)
    kpos = jnp.arange(S)

    def block(args):
        i, q_i, c_i = args
        qpos = i * Q_BLOCK + jnp.arange(Q_BLOCK)
        s = jnp.einsum("bhqd,bshd->bhqs", q_i, k,
                       preferred_element_type=jnp.float32) * scale
        s = s + c_i[..., :, None] - c[:, :, None, :]
        s = jnp.where(kpos[None, :] <= qpos[:, None], s, NEG_INF)
        p = jax.nn.softmax(s, axis=-1)
        return jnp.einsum("bhqs,bshd->bqhd", p.astype(v.dtype), v)

    out = lax.map(block, (jnp.arange(nb), q_blocks, c_blocks))
    return out.transpose(1, 0, 2, 3, 4).reshape(B, S, H, Dh)

def gated_delta_rule(q, k, v, g, beta):
    out_dtype = v.dtype
    B, S, H, Dk = q.shape
    Dv = v.shape[-1]
    C = GDN_CHUNK
    N = S // C
    f32 = jnp.float32

    def chunk(t):
        t = t.astype(f32).reshape((B, N, C, H) + t.shape[3:])
        return jnp.moveaxis(t, 3, 1)

    q = chunk(q) * (Dk ** -0.5)
    k = chunk(k)
    v = chunk(v)
    beta = chunk(beta)
    gc = jnp.cumsum(chunk(g), axis=-1)

    idx = jnp.arange(C)
    lower_incl = idx[:, None] >= idx[None, :]
    strict = idx[:, None] > idx[None, :]
    decay = jnp.exp(jnp.where(lower_incl, gc[..., :, None] - gc[..., None, :], NEG_INF))

    k_beta = k * beta[..., None]
    v_beta = v * beta[..., None]
    L = jnp.where(strict, jnp.einsum("bhncd,bhnsd->bhncs", k_beta, k) * decay, 0.0)
    eye = jnp.broadcast_to(jnp.eye(C, dtype=f32), L.shape)
    T = lax.linalg.triangular_solve(eye + L, eye, left_side=True, lower=True)
    u = jnp.einsum("bhncs,bhnse->bhnce", T, v_beta)
    w = jnp.einsum("bhncs,bhnsd->bhncd", T, k_beta * jnp.exp(gc)[..., None])
    intra = jnp.einsum("bhncd,bhnsd->bhncs", q, k) * decay

    def to_scan(t):
        return jnp.moveaxis(t, 2, 0)

    def step(state, xs):
        q_n, k_n, u_n, w_n, gc_n, intra_n = xs
        v_new = u_n - jnp.einsum("bhcd,bhde->bhce", w_n, state)
        o = (jnp.einsum("bhcd,bhde->bhce", q_n * jnp.exp(gc_n)[..., None], state)
             + jnp.einsum("bhcs,bhse->bhce", intra_n, v_new))
        g_last = gc_n[..., -1]
        state = (state * jnp.exp(g_last)[..., None, None]
                 + jnp.einsum("bhcd,bhce->bhde",
                              k_n * jnp.exp(g_last[..., None] - gc_n)[..., None], v_new))
        return state, o

    state0 = jnp.zeros((B, H, Dk, Dv), f32)
    _, o = lax.scan(step, state0, (to_scan(q), to_scan(k), to_scan(u), to_scan(w),
                                   to_scan(gc), to_scan(intra)))
    return o.transpose(1, 0, 3, 2, 4).reshape(B, S, H, Dv).astype(out_dtype)

def setup_inputs(seed: int = 0) -> dict:
    key = jax.random.key(seed)
    ks = jax.random.split(key, 26)
    L = DEPTH
    f32 = jnp.float32

    def nrm(k, shape, scale):
        return jax.random.normal(k, shape, f32) * scale

    def gain(k, dim):
        return 1.0 + 0.02 * jax.random.normal(k, (L, dim), f32)

    dt = jnp.exp(jax.random.uniform(ks[10], (L, GDN_HEADS), f32,
                                    minval=np.log(0.001), maxval=np.log(0.1)))
    return {
        "x": nrm(ks[0], (BATCH, SEQ, D_MODEL), 1.0),
        "mem": nrm(ks[1], (BATCH, MEM_LEN, D_MODEL), 1.0),
        "norm_mix_g": gain(ks[2], D_MODEL),
        "w_in": nrm(ks[3], (L, D_MODEL, IN_DIM), D_MODEL ** -0.5),
        "fox_qnorm_g": gain(ks[4], FOX_HEAD_DIM),
        "fox_knorm_g": gain(ks[5], FOX_HEAD_DIM),
        "fox_f_bias": 2.0 + 0.5 * jax.random.normal(ks[6], (L, FOX_HEADS), f32),
        "fox_onorm_g": gain(ks[7], FOX_HEAD_DIM),
        "gdn_conv_w": nrm(ks[8], (L, CONV_WIDTH, 3 * GDN_WIDTH), CONV_WIDTH ** -0.5),
        "gdn_A_log": jnp.log(jax.random.uniform(ks[9], (L, GDN_HEADS), f32, minval=1.0, maxval=16.0)),
        "gdn_dt_bias": dt + jnp.log(-jnp.expm1(-dt)),
        "gdn_onorm_g": gain(ks[11], GDN_HEAD_DIM),
        "w_out": nrm(ks[12], (L, MIX_WIDTH, D_MODEL), MIX_WIDTH ** -0.5),
        "norm_xattn_g": gain(ks[13], D_MODEL),
        "mem_norm_g": gain(ks[14], D_MODEL),
        "w_cq": nrm(ks[15], (L, D_MODEL, XATTN_WIDTH), D_MODEL ** -0.5),
        "w_ckv": nrm(ks[16], (L, D_MODEL, 2 * XATTN_WIDTH), D_MODEL ** -0.5),
        "xattn_qnorm_g": gain(ks[17], XATTN_HEAD_DIM),
        "xattn_knorm_g": gain(ks[18], XATTN_HEAD_DIM),
        "w_co": nrm(ks[19], (L, XATTN_WIDTH, D_MODEL), XATTN_WIDTH ** -0.5),
        "norm_mlp_g": gain(ks[20], D_MODEL),
        "w_mlp1": nrm(ks[21], (L, D_MODEL, D_FF), D_MODEL ** -0.5),
        "w_mlp2": nrm(ks[22], (L, D_FF, D_MODEL), D_FF ** -0.5),
    }

def reference(x, mem, norm_mix_g, w_in, fox_qnorm_g, fox_knorm_g, fox_f_bias, fox_onorm_g,
              gdn_conv_w, gdn_A_log, gdn_dt_bias, gdn_onorm_g, w_out,
              norm_xattn_g, mem_norm_g, w_cq, w_ckv, xattn_qnorm_g, xattn_knorm_g, w_co,
              norm_mlp_g, w_mlp1, w_mlp2):
    B, S, _ = x.shape
    M = mem.shape[1]
    for l in range(DEPTH):
        h = rms_norm(x, norm_mix_g[l])
        proj = h @ w_in[l]
        fox_qkv, fox_f, gdn_qkv, gdn_b, gdn_a, gdn_z = jnp.split(proj, IN_OFFSETS, axis=-1)

        fq, fk, fv = jnp.split(fox_qkv.reshape(B, S, 3 * FOX_HEADS, FOX_HEAD_DIM), 3, axis=2)
        fq = rms_norm(fq, fox_qnorm_g[l])
        fk = rms_norm(fk, fox_knorm_g[l])
        o_a = forgetting_attention(fq, fk, fv, fox_f + fox_f_bias[l])
        o_a = rms_norm(o_a, fox_onorm_g[l]).reshape(B, S, FOX_WIDTH)

        gqkv = jax.nn.silu(causal_depthwise_conv(gdn_qkv, gdn_conv_w[l]))
        gq, gk, gv = jnp.split(gqkv.reshape(B, S, 3 * GDN_HEADS, GDN_HEAD_DIM), 3, axis=2)
        gq = l2_norm(gq)
        gk = l2_norm(gk)
        beta = jax.nn.sigmoid(gdn_b.astype(jnp.float32))
        g = -jnp.exp(gdn_A_log[l].astype(jnp.float32)) * jax.nn.softplus(
            (gdn_a + gdn_dt_bias[l]).astype(jnp.float32))
        o_b = gated_delta_rule(gq, gk, gv, g, beta)
        o_b = rms_norm(o_b, gdn_onorm_g[l]) * jax.nn.silu(gdn_z.reshape(B, S, GDN_HEADS, GDN_HEAD_DIM))
        o_b = o_b.reshape(B, S, GDN_WIDTH)

        x = x + jnp.concatenate([o_a, o_b], axis=-1) @ w_out[l]

        hq = rms_norm(x, norm_xattn_g[l])
        hm = rms_norm(mem, mem_norm_g[l])
        cq = rms_norm((hq @ w_cq[l]).reshape(B, S, XATTN_HEADS, XATTN_HEAD_DIM), xattn_qnorm_g[l])
        ck, cv = jnp.split((hm @ w_ckv[l]).reshape(B, M, 2 * XATTN_HEADS, XATTN_HEAD_DIM), 2, axis=2)
        ck = rms_norm(ck, xattn_knorm_g[l])
        s = jnp.einsum("bqhd,bmhd->bhqm", cq, ck,
                       preferred_element_type=jnp.float32) * (XATTN_HEAD_DIM ** -0.5)
        p = jax.nn.softmax(s, axis=-1)
        co = jnp.einsum("bhqm,bmhd->bqhd", p.astype(cv.dtype), cv).reshape(B, S, XATTN_WIDTH)
        x = x + co @ w_co[l]

        hf = rms_norm(x, norm_mlp_g[l])
        x = x + jnp.square(jax.nn.relu(hf @ w_mlp1[l])) @ w_mlp2[l]
    return x


_drawn_inputs = setup_inputs


def setup_inputs(seed=0):
    import zlib

    import numpy as np

    out = dict(_drawn_inputs(seed))
    spreads = {}
    factors = {'fox_qnorm_g': 6.38,
     'fox_knorm_g': 5.479,
     'fox_onorm_g': 4.646,
     'gdn_onorm_g': 7.529,
     'norm_xattn_g': 8.0,
     'mem_norm_g': 8.0,
     'xattn_qnorm_g': 8.0,
     'xattn_knorm_g': 8.0,
     'norm_mlp_g': 10.775}
    for name, (base, spread) in spreads.items():
        noise = np.random.default_rng([zlib.crc32(name.encode()), seed]).standard_normal(out[name].shape)
        drawn = base * np.exp(spread * noise) if base else spread * noise
        out[name] = __import__('jax').numpy.asarray(drawn.astype(out[name].dtype))
    for name, factor in factors.items():
        out[name] = (out[name] * factor).astype(out[name].dtype)
    return out
```

```python
import math
from contextlib import ExitStack

import concourse.bass as bass
from concourse import mybir

F32 = mybir.dt.float32
F32R = mybir.dt.float32r
BF16 = mybir.dt.bfloat16
ALU = mybir.AluOpType
ACT = mybir.ActivationFunctionType
AX = mybir.AxisListType

P = 128
D = 1024
S = 1024
KT = D // P
NT = S // P
HALF = 512
FH, FD = 8, 64
GH, GD = 4, 128
XH, XD = 4, 128
MEM = 256
MT = MEM // P
DFF = 4 * D
EPS = 1e-6
ONE = 1
NEG = -1e30
GATES = FH + 2 * GH
QA = FD + 2
STEPS = GH
CONV = 4
LEVELS = 7

GK, GQ, GV, FQ, FK, FV, GZ = range(7)
STEP_TILES = 7
OUT_TILES, CK_TILES, CV_TILES, CQ_TILES, CO_TILES = KT, XH, XH, XH, KT // 2
FF_GROUPS, FF_PER = 8, 4
W2_TILES = KT // 2
T_MIX = 0
T_OUT = T_MIX + STEPS * STEP_TILES
T_CK = T_OUT + OUT_TILES
T_CV = T_CK + CK_TILES
T_CQ = T_CV + CV_TILES
T_CO = T_CQ + CQ_TILES
T_MLP = T_CO + CO_TILES
TILES = T_MLP + FF_GROUPS * (FF_PER + W2_TILES)
PHASES = [(T_MIX, STEPS, STEP_TILES), (T_OUT, (T_MLP - T_OUT) // 4, 4),
          (T_MLP, FF_GROUPS, FF_PER + W2_TILES)]

C_ID, C_TRI, C_ONE, C_M0, C_NEGF, C_NEGG = (P * n for n in range(6))
C_LV = 6 * P
C_END = C_LV + (LEVELS - 1) * (P // 2)
V_MIX, V_XAT, V_MEM, V_MLP = 0, 8, 16, 24
V_CONV = 32
V_GON, V_XQ, V_XK = 80, 81, 82
V_BIAS = 83
V_ALOG = 99
V_FQ, V_FK, V_FO = 103, 167, 231
V_END = 295

K_G, K_NGC, K_EG, K_EGL, K_EKD, K_BETA = range(6)


DEEP = False
LEAD, SPACE_PREP, SPACE_SCAN = 2.5, 1.2, 2.4
UNITS = [(0, n) for n in range(NT)] + [(1, n) for n in reversed(range(NT))]
PREPARE = ["k_in", "k_t", "kb_t", "decay", "q_in", "q_t", "qe_t", "kk", "kq", "v_in", "t_first"]


def mixer_schedule():
    tile = 4 * 2.6
    main = []

    def project(m, between=()):
        before = {GQ: 0, GV: 1, FQ: 2}.get(m)
        for q in range(4):
            main.append((("proj", m, q), tile / 4))
            if before is not None and q < 3:
                main.append((("silu", before, q), 0.0))
            main.extend(between[q:q + 1])

    for m in (GK, GQ, GV, FQ):
        project(m)
    for m, others in ((FK, [("fox_in", 0)]), (FV, [("fox_in", 1), ("fox_out", 0)]),
                      (GZ, [("fox_in", 2), ("fox_out", 1)])):
        project(m, [(o, 1.0) for o in others] if DEEP else ())
        if not DEEP:
            main += [(o, 1.0) for o in others]
    main += [(("scores", 0), 0.5)]
    for u in range(2 * NT):
        n = UNITS[u][1] + 1
        main += [(("turn", u), 0.11 * n)]
        if u + 1 < 2 * NT:
            main.append((("scores", u + 1), 0.1 + 0.43 * (UNITS[u + 1][1] + 1)))
        main += [(("values", u), 0.22 * n)]
        if u < 3:
            main.append((("silu", 3, u), 0.0))
    main += [(("fox_norm",), 1.0)]
    prep, scan = [], []
    for name in PREPARE:
        prep += [(name, h) for h in range(2)]
    for l in range(1, LEVELS):
        for name in ("lt", "tlt", "tt"):
            prep += [(name, h, l) for h in range(2)]
    for name in ("w", "u"):
        prep += [(name, h) for h in range(2)]
    for h in range(2):
        for c in range(4):
            scan += [("read", h, c), ("write", h, c)]
    fill = [(p, LEAD, SPACE_PREP) for p in prep] + [(p, LEAD, SPACE_SCAN) for p in scan]
    needs = {"k_in": ("silu", 0, 2), "q_in": ("silu", 1, 2), "v_in": ("silu", 2, 2)}
    out, now, due, at = [], 0.0, 2 * tile + LEAD, 0
    for piece, cost in main:
        if piece[0] == "turn" and at < len(fill):
            out.append(fill[at][0])
            due += fill[at][2]
            at += 1
        out.append(piece)
        now += cost
        while at < len(fill) and now >= due and needs.get(fill[at][0][0]) in [None] + out:
            out.append(fill[at][0])
            due += fill[at][2]
            at += 1
    out += [p for p, _, _ in fill[at:]]
    return out + [("gdn_norm",), ("fox_store",), ("gdn_store",)]


SCHEDULE = mixer_schedule()
TURNS = {}
for _u in range(2 * NT):
    for _g in range(UNITS[_u][1] // 4 + 1):
        TURNS[_u, _g] = len(TURNS)
N_TURNS = len(TURNS)


def build_layer(nc, xt, memt, wstream, wgate, consts, vecs, out):
    with ExitStack() as ctx:
        def sb(name, shape, dt=F32, c=ctx):
            return c.enter_context(nc.sbuf_tensor(name, shape, dt))

        def sem(name):
            return ctx.enter_context(nc.semaphore(name))

        raw = sb("raw", [P, 2, KT * P])
        w_hi = sb("w_hi", [P, 2, KT, P], F32R)
        w_lo = sb("w_lo", [P, 2, KT, P], F32R)
        h_hi = sb("h_hi", [P, KT, S], F32R)
        h_lo = sb("h_lo", [P, KT, S], F32R)
        x = sb("x", [P, KT, S])
        cst = sb("cst", [P, C_END])
        vec = sb("vec", [P, V_END])
        ident_b = sb("ident_b", [P, P], BF16)
        neg_b = sb("neg_b", [P, 2, P], BF16)
        ident, tri, ones = (cst[:, c:c + P] for c in (C_ID, C_TRI, C_ONE))
        eps_t = sb("eps_t", [P, 1])
        qbias = sb("qbias", [P, 2])

        mix = ExitStack()
        msb = lambda name, shape, dt=F32: sb(name, shape, dt, mix)
        xf = x[:, :, :].rearrange("p k s -> p (k s)")
        gk, gq, gv, gz = (xf[:, S * n:S * (n + 1)] for n in range(4))
        halves = lambda ap: [ap[:, HALF * h:HALF * (h + 1)] for h in range(2)]
        chunks = lambda aps: [ap.rearrange("p (c n) -> p c n", n=P) for ap in aps]
        kd, qeT, vb = halves(gk), halves(gq), halves(gv)
        g_in = msb("g_in", [P, CONV - 1 + S])
        silu_scratch = [gz, gz, gz, g_in[:, CONV - 1:]]
        kT, kbT, qT, decay = (halves(xf[:, S * n:S * (n + 1)]) for n in range(4, 8))
        intra, wT, u_tok = kT, kbT, chunks(qT)
        lt, tm = chunks(kbT), chunks(qT)
        kb_tok = halves(msb("kb_tok", [P, S]))
        n_tok = halves(msb("n_tok", [P, S]))
        tmT_both = halves(msb("tmT", [P, S]))
        qe_tok, tmT = tmT_both, chunks(tmT_both)
        lt_t = [ap[:, 0:4 * (P // 2)].rearrange("p (c n) -> p c n", c=4) for ap in n_tok]
        state = msb("state", [P, P])
        vnew = msb("vnew", [P, P])
        g_ss = msb("g_ss", [P, 2, 4])
        g_ln = msb("g_ln", [P, 2, 4])
        g_r = msb("g_r", [P, 2, 4])
        g_sc = msb("g_sc", [P, 6, NT])
        f_in = msb("f_in", [P, S])
        qk_tok = msb("qk_tok", [P, 2, NT, 2, QA])
        qkT = msb("qkT", [QA, 2, 2, S])
        v_tok = msb("v_tok", [P, NT, 2, FD + 1])
        probs = msb("probs", [P, 2, S])
        probsT = msb("probsT", [P, 4, HALF])
        o_tok = msb("o_tok", [P, NT, 2, FD])
        f_ss = msb("f_ss", [P, NT * 2])
        f_ln = msb("f_ln", [P, NT * 2])
        f_r = msb("f_r", [P, NT * 2])
        nmax = msb("nmax", [P, 2])
        rl = msb("rl", [P, 2])
        gain_q = msb("gain_q", [P, FD])
        gate_w = msb("gate_w", [P, KT, GATES])
        gate_hi = msb("gate_hi", [P, KT, GATES], F32R)
        gate_lo = msb("gate_lo", [P, KT, GATES], F32R)
        gates_tok = msb("gates_tok", [P, NT, GATES])
        ga = msb("ga", [P, NT, GATES])
        gb = msb("gb", [P, NT, GATES])
        glog = msb("glog", [P, NT, FH + GH])
        cum = msb("cum", [P, NT, FH + GH])
        tot = msb("tot", [P, NT, FH + GH])
        carry = msb("carry", [P, NT, FH])
        cumf = msb("cumf", [P, 2, STEPS, NT, 2])
        a_exp = msb("a_exp", [P, GH])
        gsc = msb("gsc", [P, 6, GH, NT])
        conv_taps = msb("conv_taps", [P, 3, CONV])
        conv_all = vec[:, V_CONV:V_CONV + 3 * GH * CONV].rearrange("p (t h j) -> p t h j", h=GH, j=CONV)
        mix.close()

        tail = ExitStack()
        tsb = lambda name, shape, dt=F32: sb(name, shape, dt, tail)
        part_hi = tsb("part_hi", [P, FF_PER, S], F32R)
        part_lo = tsb("part_lo", [P, FF_PER, S], F32R)
        rms = tsb("rms", [P, S])
        tmp = tsb("tmp", [P, 2, S])
        kx = tsb("kx", [P, XH, MEM])
        vx = tsb("vx", [P, XH, MT, P])
        vh = tsb("vh", [P, 2, MT, P])
        mx = tsb("mx", [P, KT * MEM])
        kv = tsb("kv", [P, 2, XH * MEM])
        xmax = tsb("xmax", [P, 4])
        xsum = tsb("xsum", [P, 4])
        xr = tsb("xr", [P, 4])
        gain_x = tsb("gain_x", [P, 1])
        tail.close()
        ps = ctx.enter_context(nc.psum_tensor("ps", [P, 8, HALF], F32))
        mixed = nc.dram_tensor("mixed", (KT, P, S), F32, kind="Internal").ap()

        consts_loaded = sem("consts_loaded")
        gatew_loaded = sem("gatew_loaded")
        x_loaded = [sem(f"x_loaded{k}") for k in range(KT)]
        raw_loaded = [sem(f"raw_loaded{s}") for s in range(2)]
        w_rounded = sem("w_rounded")
        w_split = sem("w_split")
        w_used = sem("w_used")
        gatew_rounded = sem("gatew_rounded")
        gatew_split = sem("gatew_split")
        prepared = sem("prepared")
        gained = sem("gained")
        n_sq, n_sum, n_ps, n_ln, n_rms, n_h, n_hi, n_lo = (
            sem(f"norm_{s}") for s in ("sq", "sum", "ps", "ln", "rms", "h", "hi", "lo"))
        gate_ps, gate_rows, gate_turned, gate_dve, gate_act, cum_ps, cum_read = (
            sem(s) for s in ("gate_ps", "gate_rows", "gate_turned", "gate_dve", "gate_act", "cum_ps", "cum_read"))
        proj_read = sem("proj_read")
        conv_acc = sem("conv_acc")
        conv_done = sem("conv_done")
        silu_act = sem("silu_act")
        silu_arg = sem("silu_arg")
        silu_done = sem("silu_done")
        fox_turned = sem("fox_turned")
        f_sq, f_ssd, f_lnd, f_rd, qk_scaled, q_gained, qk_cum, v_copied = (
            sem(s) for s in ("f_sq", "f_ssd", "f_lnd", "f_rd", "qk_scaled", "q_gained", "qk_cum", "v_copied"))
        qkT_turned, qkT_copied = sem("qkT_turned"), sem("qkT_copied")
        scores_ready, max_ready, probs_ready, turned, o_done, rl_ready, o_read = (
            sem(s) for s in ("scores_ready", "max_ready", "probs_ready", "turned", "o_done", "rl_ready", "o_read"))
        probT_by = [sem("probT_act"), sem("probT_dve")]
        o_sq, o_ss, o_ln, o_r, o_scaled, o_normed, o_turned, o_staged = (
            sem(s) for s in ("o_sq", "o_ss", "o_ln", "o_r", "o_scaled", "o_normed", "o_turned", "o_staged"))
        stored_f, stored_g = sem("stored_f"), sem("stored_g")
        g_full = {6: sem("g_full6"), 7: sem("g_full7")}
        g_empty = {6: sem("g_empty6"), 7: sem("g_empty7")}
        head_ready = sem("head_ready")
        g_sqd, g_ssd, g_lnd, g_rd, g_tok, g_tri, t_init = (
            [sem(f"{s}{h}") for h in range(2)] for s in ("g_sqd", "g_ssd", "g_lnd", "g_rd", "g_tok", "g_tri", "t_init"))
        gn_sq, gn_rms, gn_scaled, g_out = (sem(s) for s in ("gn_sq", "gn_rms", "gn_scaled", "g_out"))
        mixed_in = [sem("mixed_in0"), sem("mixed_in1")]
        mixed_hi, mixed_lo = sem("mixed_hi"), sem("mixed_lo")
        tail_read = sem("tail_read")
        mem_loaded = sem("mem_loaded")
        kv_squared, kv_sums, kv_ln, kx_ready, vt_copied, vx_turned, vx_ready, vh_ready = (
            sem(s) for s in ("kv_squared", "kv_sums", "kv_ln", "kx_ready", "vt_copied", "vx_turned", "vx_ready",
                             "vh_ready"))
        xq_squared, xq_sums, xq_ln, xq_rms, xq_ready, xs_ready, xmax_ready, xe_ready, xr_ready = (
            sem(s) for s in ("xq_squared", "xq_sums", "xq_ln", "xq_rms", "xq_ready", "xs_ready", "xmax_ready",
                             "xe_ready", "xr_ready"))
        xp_ready, xp_turned, xpT_act, xpT_dve, xo_done, xo_hi, xo_lo, co_even, w2_even = (
            sem(s) for s in ("xp_ready", "xp_turned", "xpT_act", "xpT_dve", "xo_done", "xo_hi", "xo_lo", "co_even",
                             "w2_even"))
        ff_relu, ff_sq, ff_hi, ff_lo = (sem(s) for s in ("ff_relu", "ff_sq", "ff_hi", "ff_lo"))
        ff_used = sem("ff_used")
        stored = sem("stored")

        use = {}
        count = {6: 0, 7: 0}
        for piece in SCHEDULE:
            if piece[0] in PREPARE + ["lt", "tlt", "tt", "w", "u"]:
                banks = [6 + piece[1]]
            else:
                banks = {"read": [6, 7], "write": [6], "gdn_norm": [6, 7]}.get(piece[0], [])
            for b in banks:
                use[piece, b] = count[b]
                count[b] += 1
        for h in range(2):
            for c in range(4):
                use[("write", h, c), 7] = use[("read", h, c), 7]

        def full(i, piece, b):
            return i * count[b] + use[piece, b] + 1

        def empty(i, piece, b):
            return ONE + i * count[b] + use[piece, b] + 1

        def free(i, piece, b):
            return ONE + i * count[b] + use[piece, b]

        def bc(ap, n):
            return ap.unsqueeze(2).to_broadcast([P, ap.shape[1], n])

        def bank2(b):
            return ps[:, b:b + 2, :].rearrange("p b n -> p (b n)")

        def flat(ap):
            return ap.rearrange("p a b -> p (a b)")

        def evens(t, l):
            return t.rearrange("p c (n two s) -> p (c n) two s", two=2, s=2 ** l)[:, :, 0, :]

        def blocks(t, l):
            return t.rearrange("p c (n s) -> p (c n) s", s=2 ** l)

        def stream_slot(phase, m):
            return (m + (phase > 0)) % 2

        def loads(phase, it, m):
            slot = stream_slot(phase, m)
            if phase == 0:
                return (4 - slot) * it + m // 2 + 1
            base = (4 - slot) * STEPS + (0 if phase == 1 else (T_MLP - T_OUT) // 2)
            return base + PHASES[phase][2] // 2 * it + m // 2 + 1


        def copy_turned(eng, copy, i, u, g):
            c = TURNS[u, g]
            width = P * (min(4 * g + 4, UNITS[u][1] + 1) - 4 * g)
            eng.wait_ge(turned, i * N_TURNS + c + 1)
            before = next((v for (v, w), d in TURNS.items() if d == c - 4), -1)
            eng.wait_ge(o_done, ONE + i * 16 + before + 1)
            copy(probsT[:, c % 4, 0:width], ps[:, 4 + c % 2, 0:width]).then_inc(probT_by[c % 2], 1)

        def norm_act(act, q, n, src, src_ready, gain, hi, lo, acc, scratch, bank):
            for k in range(KT):
                src_ready(act, k)
                if k >= 3:
                    act.wait_ge(n_sum, 7 * q + k - 2)
                nc.scalar.activation(scratch(k) if k else acc, src(k), ACT.Square).then_inc(n_sq, 1)
            act.wait_ge(n_ps, q + 1)
            for b in range(0, n, HALF):
                w = min(HALF, n - b)
                op = nc.scalar.activation(acc[:, b:b + w], ps[:, bank + b // HALF, 0:w], ACT.Ln, bias=eps_t[:, :],
                                          scale=1.0 / D)
                op.then_inc(n_ln, 1)
            act.wait_ge(n_ln, (0, 2, 3, 5, 7)[q + 1])
            nc.scalar.activation(acc, acc, ACT.Exp, scale=-0.5).then_inc(n_rms, 1)
            for k in range(KT):
                act.wait_ge(n_h, KT * q + k + 1)
                nc.scalar.copy(hi(k), scratch(k)).then_inc(n_hi, 1)

        def norm_add(dve, q, n, src, src_ready, gain, hi, lo, acc, scratch, bank):
            for k in range(1, KT):
                dve.wait_ge(n_sq, KT * q + k + 1)
                dve.wait_ge(n_sum, 7 * q + k - 1)
                nc.vector.tensor_tensor(acc, acc, scratch(k), ALU.add).then_inc(n_sum, 1)

        def norm_apply(dve, q, n, src, src_ready, gain, hi, lo, acc, scratch, bank):
            dve.wait_ge(n_rms, q + 1)
            dve.wait_ge(n_sum, 7 * q + 7)
            for k in range(KT + 1):
                if k < KT:
                    if k >= 2:
                        dve.wait_ge(n_lo, KT * q + k - 1)
                    nc.vector.scalar_tensor_tensor(scratch(k), src(k), vec[:, gain + k:gain + k + 1], acc,
                                                   ALU.mult, ALU.mult).then_inc(n_h, 1)
                if k:
                    dve.wait_ge(n_hi, KT * q + k)
                    nc.vector.tensor_tensor(lo(k - 1), scratch(k - 1), hi(k - 1).bitcast(F32), ALU.subtract
                                            ).then_inc(n_lo, 1)

        def norm_pe(pe, q, n, acc, bank):
            pe.wait_ge(n_sum, 7 * q + 7)
            for b in range(0, n, HALF):
                w = min(HALF, n - b)
                op = nc.tensor.matmul(ps[:, bank + b // HALF, 0:w], ones, acc[:, b:b + w], start=True, stop=True)
            op.then_inc(n_ps, 1)

        mix_scratch = probsT[:, :, :].rearrange("p (t a) b -> p t (a b)", t=2)
        norm_mix = (0, S, lambda k: x[:, k, :], lambda eng, k: eng.wait_ge(x_loaded[k], 16), V_MIX,
                    lambda k: h_hi[:, k, :], lambda k: h_lo[:, k, :], probs[:, 0, :],
                    lambda k: mix_scratch[:, k % 2, :], 6)
        mem_x = mx[:, :].rearrange("p (k n) -> p k n", n=MEM)
        hm_hi = part_hi[:, 0:2, :].rearrange("p a (b n) -> p (a b) n", n=MEM)
        hm_lo = part_lo[:, 0:2, :].rearrange("p a (b n) -> p (a b) n", n=MEM)
        norm_mem = (1, MEM, lambda k: mem_x[:, k, :], lambda eng, k: eng.wait_ge(mem_loaded, 16), V_MEM,
                    lambda k: hm_hi[:, k, :], lambda k: hm_lo[:, k, :], kv[:, 0, 0:MEM],
                    lambda k: kv[:, 1, MEM * (k % 2):MEM * (k % 2 + 1)], 6)

        def x_after_out(eng, k):
            eng.wait_ge(tail_read, 4 + k + 1)

        def x_after_cross(eng, k):
            eng.wait_ge(tail_read, 12 + k + 1)

        norm_xat, norm_mlp = (
            (q, S, lambda k: x[:, k, :], ready, gain, lambda k: h_hi[:, k, :], lambda k: h_lo[:, k, :],
             rms[:, :], lambda k: tmp[:, k % 2, :], 6)
            for q, ready, gain in ((2, x_after_out, V_XAT), (3, x_after_cross, V_MLP)))

        xp = mx[:, 0:4 * MEM].rearrange("p (t n) -> p t n", n=MEM)
        xpT = mx[:, 4 * MEM:].rearrange("p (t n) -> p t n", n=HALF)

        def tail_tensor(pe, split_product):
            mm = nc.tensor.matmul

            def product(slot, w0, kts, pair, hi, lo, n=S, before=None):
                for b in range(0, n, HALF):
                    for j, k in enumerate(kts):
                        if before and b == 0:
                            before(k)
                        cols = slice(b, min(b + HALF, n))
                        op = split_product(ps[:, 2 * pair + b // HALF, 0:min(HALF, n)], slot, (k,),
                                           lambda k: hi[:, k, cols], lambda k: lo[:, k, cols], n,
                                           j == 0, j == len(kts) - 1, w0=w0 + j)
                return op

            with pe.Fori(0, OUT_TILES // 4) as it:
                for j in range(4):
                    pe.wait_ge(w_split, ONE + it * 4 + T_OUT + j + 1)
                    pe.wait_ge(tail_read, it * 4 + j + 1)
                    op = product(stream_slot(1, j), 0, range(KT), j, h_hi, h_lo,
                                 before=(lambda k: pe.wait_ge(mixed_lo, k + 1)) if j == 0 else None)
                    op.then_inc(w_used, 1)
            pe.wait_ge(tail_read, 4 + OUT_TILES)
            norm_pe(pe, 1, MEM, kv[:, 0, 0:MEM], 6)
            for hd in range(XH):
                pe.wait_ge(w_split, ONE + T_CK + hd + 1)
                if hd == 0:
                    pe.wait_ge(n_ln, 3)
                product(stream_slot(1, hd), 0, range(KT), hd, hm_hi, hm_lo, MEM,
                        before=(lambda k: pe.wait_ge(n_lo, KT + k + 1)) if hd == 0 else None).then_inc(w_used, 1)
            pe.wait_ge(kv_squared, 1)
            for b in range(2):
                mm(ps[:, 2 * b + 1, :], ones, kv[:, 0, HALF * b:HALF * (b + 1)], start=True, stop=True
                   ).then_inc(kv_sums, 1)
            for hd in range(XH):
                pe.wait_ge(w_split, ONE + T_CV + hd + 1)
                pe.wait_ge(kx_ready, hd + 1)
                product(stream_slot(1, hd), 0, range(KT), hd, hm_hi, hm_lo, MEM).then_inc(w_used, 1)
            pe.wait_ge(vt_copied, XH)
            for hd in range(XH):
                for mt in range(MT):
                    n = hd * MT + mt
                    op = nc.tensor.transpose(ps[:, n // 4, P * (n % 4):P * (n % 4 + 1)],
                                             kv[:, 1, MEM * hd + P * mt:MEM * hd + P * (mt + 1)], ident)
            op.then_inc(vx_turned, 1)
            norm_pe(pe, 2, S, rms[:, :], 6)
            pe.wait_ge(vx_ready, 1)
            pe.wait_ge(n_ln, 5)
            with pe.Fori(0, XH // 2) as it:
                for j in range(2):
                    pe.wait_ge(w_split, ONE + it * 2 + T_CQ + j + 1)
                    pe.wait_ge(xq_ready, ONE + it * 2)
                    product(stream_slot(1, j), 0, range(KT), j, h_hi, h_lo,
                            before=(lambda k: pe.wait_ge(n_lo, 2 * KT + k + 1)) if j == 0 else None).then_inc(w_used, 1)
                for j in range(2):
                    pe.wait_ge(xq_squared, it * 2 + j + 1)
                    if j:
                        pe.wait_ge(xq_ln, it * 4 + 2)
                    else:
                        pe.wait_ge(xpT_act, ONE + it * 4)
                        pe.wait_ge(xpT_dve, ONE + it * 4)
                    for b in range(2):
                        mm(ps[:, 6 + b, :], ones, tmp[:, j, HALF * b:HALF * (b + 1)], start=True, stop=True
                           ).then_inc(xq_sums, 1)
                for j in range(2):
                    pe.wait_ge(xq_ready, ONE + it * 2 + j + 1)
                    for g in range(2):
                        n = it * 4 + 2 * j + g
                        pe.wait_ge(xo_lo, ONE + n)
                        for t in range(4):
                            q0 = HALF * g + P * t
                            op = mm(ps[:, 4 + t // 2, MEM * (t % 2):MEM * (t % 2 + 1)], tmp[:, j, q0:q0 + P],
                                    kx[:, bass.ds(it * 2 + j, 1), :].rearrange("p a n -> p (a n)"), start=True, stop=True)
                        op.then_inc(xs_ready, 1)
                        pe.wait_ge(xp_ready, n + 1)
                        for mt in range(MT):
                            if n is not None and mt == 0 and j == 0 and g == 0:
                                pe.wait_ge(xq_ln, it * 4 + 4)
                            for t in range(4):
                                op = nc.tensor.transpose(ps[:, 6 + mt, P * t:P * (t + 1)], xp[:, t, P * mt:P * (mt + 1)],
                                                         ident)
                            op.then_inc(xp_turned, 1)
                        pe.wait_ge(vh_ready, it * 2 + j + 1)
                        pe.wait_ge(xpT_act, ONE + n + 1)
                        pe.wait_ge(xpT_dve, ONE + n + 1)
                        for mt in range(MT):
                            op = mm(ps[:, 4, :], vh[:, j, mt, :], xpT[:, mt, :], start=(mt == 0), stop=(mt == MT - 1))
                        op.then_inc(xo_done, 1)
            pe.wait_ge(xo_lo, ONE + 2 * XH)
            with pe.Fori(0, CO_TILES // 2) as it:
                for j in range(4):
                    if j % 2 == 0:
                        pe.wait_ge(w_split, ONE + it * 2 + T_CO + j // 2 + 1)
                    pe.wait_ge(tail_read, it * 4 + 9 + j)
                    op = product(stream_slot(1, j // 2), 4 * (j % 2), range(XH), j, part_hi, part_lo)
                    op.then_inc(w_used if j % 2 else co_even, 1)
            norm_pe_wait(pe)
            norm_pe(pe, 3, S, rms[:, :], 6)
            pe.wait_ge(n_ln, 7)
            with pe.Fori(0, FF_GROUPS) as it:
                for j in range(FF_PER):
                    pe.wait_ge(w_split, ONE + it * 8 + T_MLP + j + 1)
                    pe.wait_ge(tail_read, it * 8 + 17 + j)
                    product(stream_slot(2, j), 0, range(KT), j, h_hi, h_lo,
                            before=(lambda k: pe.wait_ge(n_lo, 3 * KT + k + 1)) if j == 0 else None).then_inc(w_used, 1)
                for j in range(KT):
                    m = FF_PER + j // 2
                    if j % 2 == 0:
                        pe.wait_ge(w_split, ONE + it * 8 + T_MLP + m + 1)
                    if j < 4:
                        pe.wait_ge(ff_relu, it * 4 + j + 1)
                    else:
                        pe.wait_ge(tail_read, it * 8 + 17 + j)
                    op = product(stream_slot(2, m), 4 * (j % 2), range(FF_PER), j % 4, part_hi, part_lo,
                                 before=(lambda k: pe.wait_ge(ff_lo, ONE + it * 4 + k + 1)) if j == 0 else None)
                    op.then_inc(w_used if j % 2 else w2_even, 1)

        def norm_pe_wait(pe):
            pe.wait_ge(tail_read, 12 + KT)

        def tail_scalar(act):
            act.wait_ge(stored_f, ONE + 16 * STEPS)
            act.wait_ge(stored_g, ONE + 16 * STEPS)
            act.dma_start(mem_x, memt).then_inc(mem_loaded, 16)
            for k in range(KT):
                if k >= 2:
                    act.wait_ge(mixed_lo, k - 1)
                act.dma_start(tmp[:, k % 2, :], mixed[k]).then_inc(mixed_in[k % 2], 16)
                if k:
                    act.wait_ge(mixed_in[(k - 1) % 2], 16 * ((k - 1) // 2 + 1))
                    nc.scalar.copy(h_hi[:, k - 1, :], tmp[:, (k - 1) % 2, :]).then_inc(mixed_hi, 1)
            act.wait_ge(mixed_in[1], 16 * KT // 2)
            nc.scalar.copy(h_hi[:, KT - 1, :], tmp[:, (KT - 1) % 2, :]).then_inc(mixed_hi, 1)
            for k in range(KT):
                act.dma_start(x[:, k, :], xt[k]).then_inc(x_loaded[k], 16)
            norm_act(act, *norm_mem)
            for hd in range(XH):
                act.wait_ge(w_used, ONE + T_CK + hd + 1)
                op = nc.scalar.activation(kv[:, 0, MEM * hd:MEM * (hd + 1)], ps[:, 2 * hd, 0:MEM], ACT.Square)
            op.then_inc(kv_squared, 1)
            act.wait_ge(kv_sums, 2)
            for b in range(2):
                nc.scalar.activation(kv[:, 0, HALF * b:HALF * (b + 1)], ps[:, 2 * b + 1, :], ACT.Ln, bias=eps_t[:, :],
                                     scale=1.0 / XD).then_inc(kv_ln, 1)
            act.wait_ge(kv_ln, 2)
            nc.scalar.activation(kv[:, 0, :], kv[:, 0, :], ACT.Exp, scale=-0.5).then_inc(kv_ln, 1)
            for hd in range(XH):
                act.wait_ge(w_used, ONE + T_CV + hd + 1)
                nc.scalar.copy(kv[:, 1, MEM * hd:MEM * (hd + 1)], ps[:, 2 * hd, 0:MEM]).then_inc(vt_copied, 1)
            norm_act(act, *norm_xat)
            act.wait_ge(n_lo, 3 * KT)
            with act.Fori(0, XH // 2) as it:
                for j in range(2):
                    act.wait_ge(vx_ready, 1)
                    act.wait_ge(xo_done, ONE + it * 4)
                    nc.scalar.copy(vh[:, j, :, :], vx[:, bass.ds(it * 2 + j, 1), :, :].rearrange("p a m n -> p (a m) n")
                                   ).then_inc(vh_ready, 1)
                for j in range(2):
                    act.wait_ge(w_used, ONE + it * 2 + T_CQ + j + 1)
                    nc.scalar.activation(tmp[:, j, :], bank2(2 * j), ACT.Square).then_inc(xq_squared, 1)
                for j in range(2):
                    act.wait_ge(xq_sums, it * 4 + 2 * j + 2)
                    if j:
                        act.wait_ge(xq_ready, ONE + it * 2 + 1)
                    for b in range(2):
                        nc.scalar.activation(rms[:, HALF * b:HALF * (b + 1)], ps[:, 6 + b, :], ACT.Ln, bias=eps_t[:, :],
                                             scale=1.0 / XD).then_inc(xq_ln, 1)
                    act.wait_ge(xq_ln, it * 4 + 2 * j + 2)
                    nc.scalar.activation(rms[:, :], rms[:, :], ACT.Exp, scale=-0.5).then_inc(xq_rms, 1)
                for j in range(2):
                    for g in range(2):
                        n = it * 4 + 2 * j + g
                        act.wait_ge(xmax_ready, n + 1)
                        for t in range(4):
                            op = nc.scalar.activation(xp[:, t, :], ps[:, 4 + t // 2, MEM * (t % 2):MEM * (t % 2 + 1)],
                                                      ACT.Exp, bias=xmax[:, t:t + 1], accum_out=xsum[:, t:t + 1])
                        op.then_inc(xe_ready, 1)
                        act.wait_ge(xp_turned, n * 2 + 1)
                        nc.scalar.copy(xpT[:, 0, :], ps[:, 6, :]).then_inc(xpT_act, 1)
                        act.wait_ge(vx_ready, 1)
                        act.wait_ge(xo_done, ONE + n + 1)
                        nc.scalar.copy(part_hi[:, bass.ds(it * 2 + j, 1), HALF * g:HALF * (g + 1)
                                               ].rearrange("p a n -> p (a n)"), ps[:, 4, :]).then_inc(xo_hi, 1)
            norm_act(act, *norm_mlp)
            act.wait_ge(n_lo, 4 * KT)
            with act.Fori(0, FF_GROUPS) as it:
                for j in range(FF_PER):
                    act.wait_ge(w_used, ONE + it * 8 + T_MLP + j + 1)
                    act.wait_ge(ff_lo, ONE + it * 4 + max(j - 1, 0))
                    t = tmp[:, j % 2, :]
                    nc.scalar.activation(t, bank2(2 * j), ACT.Relu).then_inc(ff_relu, 1)
                    act.wait_ge(ff_relu, it * 4 + j + 1)
                    nc.scalar.activation(t, t, ACT.Square).then_inc(ff_sq, 1)

        def tail_vector(dve):
            tt_ = nc.vector.tensor_tensor
            dve.wait_ge(stored_f, ONE + 16 * STEPS)
            dve.wait_ge(stored_g, ONE + 16 * STEPS)
            nc.vector.memset(xr[:, :], 0.0).then_inc(tail_read, 4)
            for k in range(KT):
                dve.wait_ge(mixed_hi, k + 1)
                tt_(h_lo[:, k, :], tmp[:, k % 2, :], h_hi[:, k, :].bitcast(F32), ALU.subtract).then_inc(mixed_lo, 1)
            for k in range(KT):
                dve.wait_ge(x_loaded[k], 32)
            norm_add(dve, *norm_mem)
            with dve.Fori(0, OUT_TILES // 4) as it:
                for j in range(4):
                    dve.wait_ge(w_used, ONE + it * 4 + T_OUT + j + 1)
                    m = x[:, bass.ds(it * 4 + j, 1), :].rearrange("p a n -> p (a n)")
                    tt_(m, m, bank2(2 * j), ALU.add).then_inc(tail_read, 1)
            norm_apply(dve, *norm_mem)
            dve.wait_ge(kv_ln, 3)
            for hd in range(XH):
                tt_(kx[:, hd, :], ps[:, 2 * hd, 0:MEM], kv[:, 0, MEM * hd:MEM * (hd + 1)], ALU.mult).then_inc(kx_ready, 1)
            dve.wait_ge(vx_turned, 1)
            nc.vector.tensor_copy(vx[:, :, :, :].rearrange("p h m n -> p (h m n)"), bank2(0)).then_inc(vx_ready, 1)
            norm_add(dve, *norm_xat)
            norm_apply(dve, *norm_xat)
            nc.vector.scalar_tensor_tensor(gain_x[:, :], vec[:, V_XQ:V_XQ + 1], XD ** -0.5, vec[:, V_XK:V_XK + 1],
                                           ALU.mult, ALU.mult).then_inc(gained, 1)
            dve.wait_ge(gained, 1)
            with dve.Fori(0, XH // 2) as it:
                for j in range(2):
                    dve.wait_ge(xq_rms, it * 2 + j + 1)
                    nc.vector.scalar_tensor_tensor(tmp[:, j, :], bank2(2 * j), gain_x[:, :], rms[:, :], ALU.mult,
                                                   ALU.mult).then_inc(xq_ready, 1)
                for j in range(2):
                    for g in range(2):
                        n = it * 4 + 2 * j + g
                        dve.wait_ge(xs_ready, n + 1)
                        nc.vector.tensor_reduce(xmax[:, :], bank2(4).rearrange("p (t n) -> p t n", n=MEM), AX.X,
                                                ALU.max, negate=True).then_inc(xmax_ready, 1)
                        dve.wait_ge(xe_ready, n + 1)
                        nc.vector.reciprocal(xr[:, :], xsum[:, :]).then_inc(xr_ready, 1)
                        dve.wait_ge(xr_ready, n + 1)
                        tt_(xp, xp, bc(xr[:, :], MEM), ALU.mult).then_inc(xp_ready, 1)
                        dve.wait_ge(xp_turned, n * 2 + 2)
                        nc.vector.tensor_copy(xpT[:, 1, :], ps[:, 7, :]).then_inc(xpT_dve, 1)
                        dve.wait_ge(xo_hi, n + 1)
                        cols = slice(HALF * g, HALF * (g + 1))
                        at = bass.ds(it * 2 + j, 1)
                        tt_(part_lo[:, at, cols].rearrange("p a n -> p (a n)"), ps[:, 4, :],
                            part_hi[:, at, cols].rearrange("p a n -> p (a n)").bitcast(F32), ALU.subtract
                            ).then_inc(xo_lo, 1)
            with dve.Fori(0, CO_TILES // 2) as it:
                for j in range(4):
                    if j % 2:
                        dve.wait_ge(w_used, ONE + it * 2 + T_CO + j // 2 + 1)
                    else:
                        dve.wait_ge(co_even, it * 2 + j // 2 + 1)
                    m = x[:, bass.ds(it * 4 + j, 1), :].rearrange("p a n -> p (a n)")
                    tt_(m, m, bank2(2 * j), ALU.add).then_inc(tail_read, 1)
            norm_add(dve, *norm_mlp)
            norm_apply(dve, *norm_mlp)
            with dve.Fori(0, FF_GROUPS) as it:
                for j in range(FF_PER):
                    dve.wait_ge(ff_sq, it * 4 + j + 1)
                    if j == 0:
                        dve.wait_ge(w_used, ONE + it * 8 + T_MLP)
                    nc.vector.tensor_copy(part_hi[:, j, :], tmp[:, j % 2, :]).then_inc(ff_hi, 1)
                    dve.wait_ge(ff_hi, it * 4 + j + 1)
                    tt_(part_lo[:, j, :], tmp[:, j % 2, :], part_hi[:, j, :].bitcast(F32), ALU.subtract).then_inc(ff_lo, 1)
                for j in range(KT):
                    if j % 2:
                        dve.wait_ge(w_used, ONE + it * 8 + T_MLP + FF_PER + j // 2 + 1)
                    else:
                        dve.wait_ge(w2_even, it * 4 + j // 2 + 1)
                    dve.wait_ge(tail_read, it * 8 + 20)
                    tt_(x[:, j, :], x[:, j, :], bank2(2 * (j % 4)), ALU.add).then_inc(tail_read, 1)

        block = ctx.enter_context(nc.Block())

        @block.sync
        def _(sp):
            sp.dma_start(cst[:, :], consts).then_inc(consts_loaded, 16)
            sp.dma_start(vec[:, :], vecs).then_inc(consts_loaded, 16)
            for k in range(KT):
                sp.dma_start(x[:, k, :], xt[k]).then_inc(x_loaded[k], 16)
            sp.dma_start(gate_w[:, :, :], wgate).then_inc(gatew_loaded, 16)
            for phase, (first, turns, per) in enumerate(PHASES):
                with sp.Fori(0, turns) as it:
                    for m in range(per):
                        t = it * per + first + m
                        slot = stream_slot(phase, m)
                        sp.wait_ge(w_split, ONE + (t if phase == 0 and m == 0 else t - 1))
                        sp.dma_start(raw[:, slot, :], wstream[bass.ds(t, 1)].rearrange("a p n -> (a p) n")
                                     ).then_inc(raw_loaded[slot], 16)
            for k in range(KT):
                sp.wait_ge(tail_read, 12 + KT + (FF_GROUPS - 1) * KT + k + 1)
                sp.dma_start(out[k], x[:, k, :]).then_inc(stored, 16)
            sp.wait_ge(stored, 16 * KT)

        @block.gpsimd
        def _(pool):
            for s in (w_split, w_used, o_read, conv_done, silu_done, o_staged, o_done, g_empty[6], g_empty[7], xq_ready, xo_lo,
                      xo_done, ff_lo, xpT_act, xpT_dve, stored_f, stored_g):
                pool.sem_inc(s, ONE)
            pool.wait_ge(gatew_loaded, 16)
            nc.gpsimd.tensor_scalar(gate_hi[:, :, :], gate_w[:, :, :], 1.0, 1.0, ALU.mult, ALU.mult
                                    ).then_inc(gatew_rounded, 1)
            pool.wait_ge(gatew_rounded, 1)
            nc.gpsimd.tensor_tensor(gate_lo[:, :, :], gate_w[:, :, :], gate_hi[:, :, :].bitcast(F32),
                                    ALU.subtract).then_inc(gatew_split, 1)
            for phase, (first, turns, per) in enumerate(PHASES):
                with pool.Fori(0, turns) as it:
                    for m in range(per):
                        t = it * per + first + m
                        slot = stream_slot(phase, m)
                        pool.wait_ge(w_used, ONE + (t if phase == 0 and m == 0 else t - 1))
                        pool.wait_ge(raw_loaded[slot], 16 * loads(phase, it, m))
                        pool.nop(nofuse=True)
                        nc.gpsimd.tensor_scalar(flat(w_hi[:, slot, :, :]), raw[:, slot, :], 1.0, 1.0,
                                                ALU.mult, ALU.mult).then_inc(w_rounded, 1)
                        pool.wait_ge(w_rounded, t + 1)
                        nc.gpsimd.tensor_tensor(flat(w_lo[:, slot, :, :]), raw[:, slot, :],
                                                flat(w_hi[:, slot, :, :]).bitcast(F32),
                                                ALU.subtract).then_inc(w_split, 1)

        @block.tensor
        def _(pe):
            mm = nc.tensor.matmul

            def split_product(dst, slot, kts, rhs_hi, rhs_lo, n, first, last, w0=0):
                for j, k in enumerate(kts):
                    for a, (w, r) in enumerate(((w_hi, rhs_hi), (w_hi, rhs_lo), (w_lo, rhs_hi))):
                        op = mm(dst, w[:, slot, w0 + j, :], r(k), start=(first and j == 0 and a == 0),
                                stop=(last and j == len(kts) - 1 and a == 2))
                return op

            pe.wait_ge(consts_loaded, 32)
            norm_pe(pe, 0, S, probs[:, 0, :], 6)

            pe.wait_ge(gatew_split, 1)
            for k in range(KT):
                pe.wait_ge(n_lo, k + 1)
                for b in range(2):
                    cols = slice(HALF * b, HALF * (b + 1))
                    for a, (w, r) in enumerate(((gate_hi, h_hi), (gate_hi, h_lo), (gate_lo, h_hi))):
                        op = mm(ps[0:GATES, b, :], w[:, k, :], r[:, k, cols],
                                start=(k == 0 and a == 0), stop=(k == KT - 1 and a == 2))
            op.then_inc(gate_ps, 1)
            pe.wait_ge(gate_rows, 1)
            for n in range(NT):
                op = nc.tensor.transpose(ps[:, 2, GATES * n:GATES * (n + 1)], f_in[0:GATES, P * n:P * (n + 1)],
                                         ident[0:GATES, 0:GATES])
            op.then_inc(gate_turned, 1)
            pe.wait_ge(gate_dve, 5)
            mm(ps[:, 3, 0:NT * (FH + GH)], tri, flat(glog[:, :, :]), start=True, stop=True)
            mm(ps[:, 4, 0:NT * (FH + GH)], ones, flat(glog[:, :, :]), start=True, stop=True).then_inc(cum_ps, 1)
            pe.wait_ge(cum_read, 2)
            pe.wait_ge(prepared, 1)

            def fox_store(i):
                pe.wait_ge(o_normed, i + 1)
                for b in range(2):
                    pe.wait_ge(probT_by[b], (i + 1) * (N_TURNS // 2))
                for n in range(NT):
                    op = nc.tensor.transpose(ps[:, 4 + n // 4, P * (n % 4):P * (n % 4 + 1)],
                                             flat(o_tok[:, n, :, :]), ident)
                op.then_inc(o_turned, 1)

            def gdn_norm(i):
                pe.wait_ge(gn_sq, i + 1)
                for b in range(2):
                    pe.wait_ge(g_empty[6 + b], free(i, ("gdn_norm",), 6 + b))
                    mm(ps[:, 6 + b, :], ones, gk[:, HALF * b:HALF * (b + 1)], start=True, stop=True
                       ).then_inc(g_full[6 + b], 1)

            def mixer_step(i, first):
                def proj(m, q):
                    t = i * STEP_TILES + m
                    if q == 0:
                        pe.wait_ge(w_split, ONE + t + 1)
                        if m < 2:
                            pe.wait_ge(o_read, ONE + i * 16)
                        else:
                            pe.wait_ge(proj_read, i * STEP_TILES + m - 1)
                    for b in range(2):
                        cols = slice(HALF * b, HALF * (b + 1))
                        op = split_product(ps[:, 2 * (m % 2) + b, :], m % 2, (2 * q, 2 * q + 1),
                                           lambda k: h_hi[:, k, cols], lambda k: h_lo[:, k, cols], HALF,
                                           q == 0, q == 3, w0=2 * q)
                    if q == 3:
                        op.then_inc(w_used, 1)

                def silu(c, part):
                    pass

                def fox_in(t):
                    pe.wait_ge(proj_read, i * STEP_TILES + FQ + t + 1)
                    if t == 0:
                        pe.wait_ge(o_staged, ONE + i)
                    elif t == 1:
                        pe.wait_ge(qk_scaled, i * 2 + 1)
                    else:
                        pe.wait_ge(qkT_copied, i * 4 + 2)
                    for n in range(NT):
                        op = nc.tensor.transpose(ps[:, 4 + n // 4, P * (n % 4):P * (n % 4 + 1)],
                                                 f_in[:, P * n:P * (n + 1)], ident)
                    op.then_inc(fox_turned, 1)

                def fox_out(t):
                    pe.wait_ge(qk_cum, i * 2 + 2)
                    if t == 0:
                        pe.wait_ge(q_gained, i + 1)
                        pe.wait_ge(qk_scaled, i * 2 + 2)
                    else:
                        pe.wait_ge(v_copied, i + 1)
                    for hh in range(2):
                        if hh:
                            pe.wait_ge(qkT_copied, i * 4 + 2 * t + 1)
                        for n in range(NT):
                            op = nc.tensor.transpose(ps[0:QA, 4 + n // 4, P * (n % 4):P * (n % 4 + 1)],
                                                     qk_tok[:, t, n, hh, :], ident)
                        op.then_inc(qkT_turned, 1)

                def scores(u):
                    hh, n = UNITS[u]
                    b0 = 2 * (u % 2)
                    if u == 0:
                        pe.wait_ge(qkT_copied, i * 4 + 4)
                        pe.wait_ge(proj_read, i * STEP_TILES + 7)
                    if u >= 2:
                        pe.wait_ge(o_read, ONE + i * 16 + u - 1)
                    width = P * (n + 1)
                    for b in range(n // 4 + 1):
                        w = min(HALF, width - HALF * b)
                        mm(ps[:, b0 + b, 0:w], qkT[0:QA, 0, hh, P * n:P * (n + 1)],
                           qkT[0:QA, 1, hh, HALF * b:HALF * b + w], start=True, stop=True)
                    mm(ps[:, b0 + n // 4, w - P:w], ident_b[:, :], neg_b[:, 0, :], start=False, stop=True,
                       skip_group_check=True).then_inc(scores_ready, 1)

                def turn(u):
                    for g in range(UNITS[u][1] // 4 + 1):
                        c = TURNS[u, g]
                        pe.wait_ge(probs_ready, i * N_TURNS + c + 1)
                        if c >= 2:
                            pe.wait_ge(probT_by[c % 2], i * (N_TURNS // 2) + c // 2)
                        elif c == 0:
                            pe.wait_ge(qkT_copied, i * 4 + 4)
                        for j in range(4 * g, min(4 * g + 4, UNITS[u][1] + 1)):
                            op = nc.tensor.transpose(ps[:, 4 + c % 2, P * (j % 4):P * (j % 4 + 1)],
                                                     probs[:, u % 2, P * j:P * (j + 1)], ident)
                        op.then_inc(turned, 1)

                def values(u):
                    hh, n = UNITS[u]
                    for g in range(n // 4 + 1):
                        c = TURNS[u, g]
                        pe.wait_ge(probT_by[c % 2], i * (N_TURNS // 2) + c // 2 + 1)
                        for j in range(4 * g, min(4 * g + 4, n + 1)):
                            op = mm(ps[:, 2 * (u % 2), 0:FD + 1], probsT[:, c % 4, P * (j % 4):P * (j % 4 + 1)],
                                    v_tok[:, j, hh, :], start=(j == 0), stop=(j == n))
                    op.then_inc(o_done, 1)

                def turn4(piece, b, src):
                    pe.wait_ge(g_empty[b], free(i, piece, b))
                    for c in range(4):
                        op = nc.tensor.transpose(ps[:, b, P * c:P * (c + 1)], src(c), ident)
                    op.then_inc(g_full[b], 1)

                def times4(piece, b, lhs, rhs, n):
                    pe.wait_ge(g_empty[b], free(i, piece, b))
                    for c in range(4):
                        op = mm(ps[:, b, n * c:n * (c + 1)], lhs(c), rhs(c), start=True, stop=True)
                    op.then_inc(g_full[b], 1)

                def chunk(ap):
                    return lambda c: ap[:, P * c:P * (c + 1)]

                def k_in(h):
                    pe.wait_ge(silu_done, ONE + i * 4 + 1)
                    turn4(("k_in", h), 6 + h, chunk(gk[:, HALF * h:HALF * (h + 1)]))

                def k_t(h):
                    pe.wait_ge(g_empty[6 + h], empty(i, ("k_in", h), 6 + h))
                    turn4(("k_t", h), 6 + h, chunk(n_tok[h]))

                def kb_t(h):
                    pe.wait_ge(g_tok[h], i * 4 + 1)
                    turn4(("kb_t", h), 6 + h, chunk(kb_tok[h]))

                def q_in(h):
                    pe.wait_ge(silu_done, ONE + i * 4 + 2)
                    turn4(("q_in", h), 6 + h, chunk(gq[:, HALF * h:HALF * (h + 1)]))

                def q_t(h):
                    pe.wait_ge(g_empty[6 + h], empty(i, ("q_in", h), 6 + h))
                    turn4(("q_t", h), 6 + h, chunk(n_tok[h]))

                def qe_t(h):
                    pe.wait_ge(g_tok[h], i * 4 + 4)
                    turn4(("qe_t", h), 6 + h, chunk(qe_tok[h]))

                def v_in(h):
                    pe.wait_ge(silu_done, ONE + i * 4 + 3)
                    turn4(("v_in", h), 6 + h, chunk(gv[:, HALF * h:HALF * (h + 1)]))

                def decay_(h):
                    piece, b = ("decay", h), 6 + h
                    pe.wait_ge(g_empty[b], free(i, piece, b))
                    pe.wait_ge(g_tri[h], i + 1)
                    mm(ps[:, b, :], ones, decay[h], start=True, stop=True)
                    for c in range(4):
                        op = mm(ps[:, b, P * c:P * (c + 1)], ident_b[:, :], neg_b[:, 1, :], start=False,
                                stop=True, skip_group_check=True)
                    op.then_inc(g_full[b], 1)

                def kk(h):
                    times4(("kk", h), 6 + h, chunk(kT[h]), chunk(kbT[h]), P)

                def kq(h):
                    times4(("kq", h), 6 + h, chunk(kT[h]), chunk(qT[h]), P)

                def t_first(h):
                    pe.wait_ge(t_init[h], i * 2 + 2)
                    turn4(("t_first", h), 6 + h, lambda c: tmT[h][:, c, :])

                def lt_(h, l):
                    s = 2 ** l
                    times4(("lt", h, l), 6 + h, lambda c: lt[h][:, c, :],
                           lambda c: tm[h][:, c, :].rearrange("p (n two s) -> p n two s", two=2, s=s)[:, :, 0, :],
                           P // 2)

                def tlt(h, l):
                    times4(("tlt", h, l), 6 + h, lambda c: tmT[h][:, c, :], lambda c: lt_t[h][:, c, :], P // 2)

                def tt(h, l):
                    turn4(("tt", h, l), 6 + h, lambda c: tm[h][:, c, :])

                def w_(h):
                    times4(("w", h), 6 + h, chunk(kb_tok[h]), lambda c: tmT[h][:, c, :], P)

                def u_(h):
                    times4(("u", h), 6 + h, lambda c: tmT[h][:, c, :], chunk(vb[h]), P)

                def read(h, c):
                    piece = ("read", h, c)
                    if c == 0:
                        pe.wait_ge(g_empty[6 + h], empty(i, ("w", h), 6 + h))
                    pe.wait_ge(g_empty[6], free(i, piece, 6))
                    mm(ps[:, 6, 0:P], wT[h][:, P * c:P * (c + 1)], state[:, :], start=True, stop=True
                       ).then_inc(g_full[6], 1)
                    pe.wait_ge(g_empty[7], free(i, piece, 7))
                    mm(ps[:, 7, 0:P], state[:, :], qeT[h][:, P * c:P * (c + 1)], start=True, stop=False)

                def write(h, c):
                    pe.wait_ge(g_empty[6], empty(i, ("read", h, c), 6))
                    mm(ps[:, 6, 0:P], kd[h][:, P * c:P * (c + 1)], vnew[:, :], start=True, stop=True
                       ).then_inc(g_full[6], 1)
                    mm(ps[:, 7, 0:P], vnew[:, :], intra[h][:, P * c:P * (c + 1)], start=False, stop=True
                       ).then_inc(g_full[7], 1)

                step = {"proj": proj, "silu": silu, "fox_in": fox_in, "fox_out": fox_out, "scores": scores, "turn": turn,
                        "values": values, "k_in": k_in,
                        "k_t": k_t, "kb_t": kb_t, "q_in": q_in, "q_t": q_t, "qe_t": qe_t, "v_in": v_in,
                        "decay": decay_, "kk": kk,
                        "kq": kq, "t_first": t_first, "lt": lt_, "tlt": tlt, "tt": tt, "w": w_, "u": u_,
                        "read": read, "write": write}
                for name, *args in SCHEDULE:
                    if name in step:
                        step[name](*args)
                    if not first and (name, *args) == ("proj", GK, 1):
                        gdn_norm(i - 1)
                    elif not first and (name, *args) == ("proj", GK, 2):
                        fox_store(i - 1)

            mixer_step(0, True)
            with pe.Fori(1, STEPS) as i:
                mixer_step(i, False)
            gdn_norm(STEPS - 1)
            fox_store(STEPS - 1)
            tail_tensor(pe, split_product)

        @block.scalar
        def _(act):
            nc.scalar.preload_act_table_set("natural_log_exp_and_others")
            norm_act(act, *norm_mix)

            act.wait_ge(gate_ps, 1)
            nc.scalar.copy(f_in[0:GATES, :], bank2(0)[0:GATES, :]).then_inc(gate_rows, 1)
            act.wait_ge(gate_dve, 1)
            nc.scalar.activation(flat(ga[:, :, :]), flat(gates_tok[:, :, :]), ACT.Abs).then_inc(gate_act, 1)
            act.wait_ge(gate_act, 1)
            nc.scalar.activation(flat(ga[:, :, :]), flat(ga[:, :, :]), ACT.Exp, scale=-1.0).then_inc(gate_act, 1)
            act.wait_ge(gate_act, 2)
            nc.scalar.activation(flat(ga[:, :, :]), flat(ga[:, :, :]), ACT.Ln, bias=1.0).then_inc(gate_act, 1)
            nc.scalar.activation(a_exp[:, :], vec[:, V_ALOG:V_ALOG + GH], ACT.Exp).then_inc(gate_act, 1)
            act.wait_ge(gate_dve, 3)
            nc.scalar.activation(gsc[:, K_BETA, :, :], gb[:, :, FH:FH + GH].rearrange("p n g -> p g n"), ACT.Exp
                                 ).then_inc(gate_act, 1)
            act.wait_ge(gate_dve, 6)
            for kind, src in ((K_EG, cum), (K_EGL, tot), (K_EKD, glog)):
                nc.scalar.activation(gsc[:, kind, :, :], src[:, :, FH:].rearrange("p n g -> p g n"), ACT.Exp
                                     ).then_inc(gate_act, 1)

            with act.Fori(0, STEPS) as i:
                def proj(m, q):
                    if q < 3:
                        return
                    act.wait_ge(w_used, ONE + i * STEP_TILES + m + 1)
                    src = bank2(2 * (m % 2))
                    if m in (GK, GQ, GV):
                        c = (GK, GQ, GV).index(m)
                        act.wait_ge(conv_done, ONE + i * 3 + c)
                        nc.scalar.copy(g_in[:, CONV - 1:], src).then_inc(proj_read, 1)
                    elif m == GZ:
                        act.wait_ge(silu_done, ONE + i * 4 + 3)
                        act.wait_ge(stored_g, ONE + i * 16)
                        nc.scalar.copy(gz, src).then_inc(proj_read, 1)
                    else:
                        if m == FQ:
                            act.wait_ge(stored_f, ONE + i * 16)
                        else:
                            act.wait_ge(fox_turned, i * 3 + m - FQ)
                        nc.scalar.copy(f_in[:, :], src).then_inc(proj_read, 1)

                def silu(c, part):
                    dst, t = (gk, gq, gv, gz)[c], silu_scratch[c]
                    if part == 0:
                        if c < 3:
                            act.wait_ge(conv_done, ONE + i * 3 + c + 1)
                            act.wait_ge(silu_done, ONE + i * 4 + c)
                            act.wait_ge(stored_g, ONE + i * 16)
                        else:
                            act.wait_ge(proj_read, i * STEP_TILES + GZ + 1)
                            act.wait_ge(conv_done, ONE + i * 3 + 3)
                        nc.scalar.activation(t, dst, ACT.Abs).then_inc(silu_act, 1)
                        act.wait_ge(silu_act, i * 16 + c * 4 + 1)
                        nc.scalar.activation(t, t, ACT.Exp, scale=-1.0).then_inc(silu_act, 1)
                        act.wait_ge(silu_act, i * 16 + c * 4 + 2)
                        nc.scalar.activation(t, t, ACT.Ln, bias=1.0).then_inc(silu_act, 1)
                    elif part == 1:
                        act.wait_ge(silu_arg, i * 4 + c + 1)
                        nc.scalar.activation(t, t, ACT.Exp).then_inc(silu_act, 1)

                def rsqrt16(scale, done_ss, done_ln, done_r, n):
                    act.wait_ge(done_ss, n)
                    nc.scalar.activation(f_ln[:, :], f_ss[:, :], ACT.Ln, bias=eps_t[:, :], scale=scale).then_inc(done_ln, 1)
                    act.wait_ge(done_ln, n)
                    nc.scalar.activation(f_r[:, :], f_ln[:, :], ACT.Exp, scale=-0.5).then_inc(done_r, 1)

                def fox_in(t):
                    act.wait_ge(fox_turned, i * 3 + t + 1)
                    if t == 2:
                        nc.scalar.copy(v_tok[:, :, :, 0:FD], bank2(4).rearrange("p (n h d) -> p n h d", h=2, d=FD)
                                       ).then_inc(v_copied, 1)
                        return
                    if t == 1:
                        act.wait_ge(f_ssd, i * 2 + 1)
                    nc.scalar.activation(o_tok[:, :, :, :].rearrange("p n h d -> p (n h d)"), bank2(4), ACT.Square
                                         ).then_inc(f_sq, 1)
                    rsqrt16(1.0 / FD, f_ssd, f_lnd, f_rd, i * 2 + t + 1)

                def fox_out(t):
                    for hh in range(2):
                        act.wait_ge(qkT_turned, i * 4 + 2 * t + hh + 1)
                        nc.scalar.copy(qkT[:, t, hh, :], bank2(4)[0:QA, :]).then_inc(qkT_copied, 1)

                def scores(u):
                    pass

                def turn(u):
                    act.wait_ge(max_ready, i * 16 + u + 1)
                    for g in range(UNITS[u][1] // 4 + 1):
                        cols = slice(HALF * g, min(HALF * (g + 1), P * (UNITS[u][1] + 1)))
                        nc.scalar.activation(probs[:, u % 2, cols], bank2(2 * (u % 2))[:, cols], ACT.Exp,
                                             bias=nmax[:, u % 2:u % 2 + 1]).then_inc(probs_ready, 1)
                    for g in range(UNITS[u][1] // 4 + 1):
                        c = TURNS[u, g]
                        if c % 2 == 0:
                            copy_turned(act, nc.scalar.copy, i, u, g)

                def values(u):
                    pass

                def fox_norm():
                    act.wait_ge(o_read, ONE + i * 16 + 16)
                    nc.scalar.activation(f_in[:, :], o_tok[:, :, :, :].rearrange("p n h d -> p (n h d)"), ACT.Square
                                         ).then_inc(o_sq, 1)
                    rsqrt16(1.0 / FD, o_ss, o_ln, o_r, i + 1)

                def fox_store():
                    act.wait_ge(o_turned, i + 1)
                    nc.scalar.copy(f_in[:, :], bank2(4)).then_inc(o_staged, 1)
                    act.wait_ge(o_staged, ONE + i + 1)
                    act.dma_start(mixed[bass.ds(i, 1)].rearrange("a p n -> (a p) n"), f_in[:, :]).then_inc(stored_f, 16)

                def rsqrt4(h, n, bias):
                    act.wait_ge(g_ssd[h], n)
                    nc.scalar.activation(g_ln[:, h, :], g_ss[:, h, :], ACT.Ln, bias=eps_t[:, :]).then_inc(g_lnd[h], 1)
                    act.wait_ge(g_lnd[h], n)
                    nc.scalar.activation(g_r[:, h, :], g_ln[:, h, :], ACT.Exp, scale=-0.5, bias=bias).then_inc(g_rd[h], 1)

                def k_in(h):
                    act.wait_ge(g_full[6 + h], full(i, ("k_in", h), 6 + h))
                    nc.scalar.activation(n_tok[h], ps[:, 6 + h, :], ACT.Square).then_inc(g_sqd[h], 1)
                    rsqrt4(h, i * 2 + 1, 0.0)

                def q_in(h):
                    act.wait_ge(g_full[6 + h], full(i, ("q_in", h), 6 + h))
                    nc.scalar.activation(qe_tok[h], ps[:, 6 + h, :], ACT.Square).then_inc(g_sqd[h], 1)
                    rsqrt4(h, i * 2 + 2, qbias[:, 0:1])

                def copy_out(piece, b, dst):
                    act.wait_ge(g_full[b], full(i, piece, b))
                    nc.scalar.copy(dst, ps[:, b, :]).then_inc(g_empty[b], 1)

                def k_t(h):
                    copy_out(("k_t", h), 6 + h, kT[h])

                def kb_t(h):
                    copy_out(("kb_t", h), 6 + h, kbT[h])

                def q_t(h):
                    copy_out(("q_t", h), 6 + h, qT[h])

                def qe_t(h):
                    copy_out(("qe_t", h), 6 + h, qeT[h])

                def decay_(h):
                    b = 6 + h
                    act.wait_ge(g_full[b], full(i, ("decay", h), b))
                    for c in range(4):
                        op = nc.scalar.activation(decay[h][:, P * c:P * (c + 1)], ps[:, b, P * c:P * (c + 1)], ACT.Exp,
                                                  bias=g_sc[:, K_NGC, 4 * h + c:4 * h + c + 1])
                    op.then_inc(g_empty[b], 1)

                def t_first(h):
                    copy_out(("t_first", h), 6 + h, qT[h])

                def tt(h, l):
                    copy_out(("tt", h, l), 6 + h, tmT_both[h])

                def w_(h):
                    copy_out(("w", h), 6 + h, wT[h])

                def write(h, c):
                    act.wait_ge(g_full[7], full(i, ("write", h, c), 7))
                    nc.scalar.copy(gv[:, HALF * h + P * c:HALF * h + P * (c + 1)], ps[:, 7, 0:P]).then_inc(g_empty[7], 1)

                def gdn_norm():
                    act.wait_ge(g_empty[7], free(i, ("gdn_norm",), 7))
                    act.wait_ge(g_empty[6], free(i, ("gdn_norm",), 6))
                    nc.scalar.activation(gk, gv, ACT.Square).then_inc(gn_sq, 1)
                    for b in range(2):
                        act.wait_ge(g_full[6 + b], full(i, ("gdn_norm",), 6 + b))
                        nc.scalar.activation(gq[:, HALF * b:HALF * (b + 1)], ps[:, 6 + b, :], ACT.Ln, bias=eps_t[:, :],
                                             scale=1.0 / GD).then_inc(g_empty[6 + b], 1)
                    for b in range(2):
                        act.wait_ge(g_empty[6 + b], ONE + i * count[6 + b] + count[6 + b])
                    nc.scalar.activation(gq, gq, ACT.Exp, scale=-0.5).then_inc(gn_rms, 1)

                def gdn_store():
                    act.wait_ge(g_out, i + 1)
                    act.dma_start(mixed[bass.ds(i + STEPS, 1)].rearrange("a p n -> (a p) n"), gz).then_inc(stored_g, 16)

                step = {"proj": proj, "silu": silu, "fox_in": fox_in, "fox_out": fox_out, "scores": scores, "turn": turn,
                        "values": values, "fox_norm": fox_norm, "fox_store": fox_store, "k_in": k_in,
                        "k_t": k_t, "kb_t": kb_t, "q_in": q_in, "q_t": q_t, "qe_t": qe_t, "decay": decay_, "t_first": t_first,
                        "tt": tt, "w": w_, "write": write, "gdn_norm": gdn_norm, "gdn_store": gdn_store}
                for name, *args in SCHEDULE:
                    if name in step:
                        step[name](*args)
            tail_scalar(act)

        @block.vector
        def _(dve):
            tt_ = nc.vector.tensor_tensor
            ts_ = nc.vector.tensor_scalar
            stt = nc.vector.scalar_tensor_tensor
            dve.wait_ge(consts_loaded, 32)
            nc.vector.memset(eps_t[:, :], EPS)
            nc.vector.memset(qbias[:, 0:1], -0.5 * math.log(GD))
            nc.vector.memset(qk_tok[:, 0, :, :, FD:FD + 1], 1.0)
            nc.vector.memset(qk_tok[:, 1, :, :, FD + 1:QA], 1.0)
            nc.vector.memset(v_tok[:, :, :, FD:FD + 1], 1.0)
            nc.vector.memset(g_in[:, 0:CONV - 1], 0.0)
            nc.vector.tensor_copy(neg_b[:, 0, :], cst[:, C_NEGF:C_NEGF + P])
            nc.vector.tensor_copy(neg_b[:, 1, :], cst[:, C_NEGG:C_NEGG + P])
            stt(gain_q[:, :], vec[:, V_FQ:V_FQ + FD], FD ** -0.5, vec[:, V_FK:V_FK + FD], ALU.mult, ALU.mult)
            nc.vector.tensor_copy(ident_b[:, :], ident).then_inc(prepared, 1)
            norm_add(dve, *norm_mix)
            norm_apply(dve, *norm_mix)

            dve.wait_ge(gate_turned, 1)
            tt_(gates_tok[:, :, :], ps[:, 2, 0:NT * GATES].rearrange("p (n g) -> p n g", g=GATES),
                vec[:, V_BIAS:V_BIAS + GATES].unsqueeze(1).to_broadcast([P, NT, GATES]), ALU.add).then_inc(gate_dve, 1)
            dve.wait_ge(gate_act, 3)
            dve.wait_ge(gate_dve, 1)
            stt(flat(gb[:, :, :]), flat(gates_tok[:, :, :]), 0.0, flat(ga[:, :, :]), ALU.min, ALU.subtract).then_inc(gate_dve, 1)
            dve.wait_ge(gate_dve, 2)
            nc.vector.tensor_copy(glog[:, :, 0:FH], gb[:, :, 0:FH]).then_inc(gate_dve, 1)
            stt(gates_tok[:, :, FH + GH:], gates_tok[:, :, FH + GH:], 0.0, ga[:, :, FH + GH:], ALU.max, ALU.add
                ).then_inc(gate_dve, 1)
            dve.wait_ge(gate_dve, 4)
            dve.wait_ge(gate_act, 4)
            stt(glog[:, :, FH:], gates_tok[:, :, FH + GH:], -1.0,
                a_exp[:, :].unsqueeze(1).to_broadcast([P, NT, GH]), ALU.mult, ALU.mult).then_inc(gate_dve, 1)
            dve.wait_ge(gate_dve, 5)
            nc.vector.tensor_copy(gsc[:, K_G, :, :], glog[:, :, FH:].rearrange("p n g -> p g n"))
            dve.wait_ge(cum_ps, 1)
            nc.vector.tensor_copy(flat(cum[:, :, :]), ps[:, 3, 0:NT * (FH + GH)]).then_inc(cum_read, 1)
            nc.vector.tensor_copy(flat(tot[:, :, :]), ps[:, 4, 0:NT * (FH + GH)]).then_inc(cum_read, 1)
            dve.wait_ge(cum_read, 2)
            tt_(glog[:, :, FH:], tot[:, :, FH:], cum[:, :, FH:], ALU.subtract).then_inc(gate_dve, 1)
            ts_(gsc[:, K_NGC, :, :], cum[:, :, FH:].rearrange("p n g -> p g n"), -1.0, None, ALU.mult)
            nc.vector.memset(carry[:, 0, :], 0.0).then_inc(gate_dve, 1)
            for n in range(1, NT):
                dve.wait_ge(gate_dve, 6 + n)
                tt_(carry[:, n, :], carry[:, n - 1, :], tot[:, n - 1, 0:FH], ALU.add).then_inc(gate_dve, 1)
            dve.wait_ge(gate_dve, 6 + NT)
            pairs = lambda t: t[:, :, 0:FH].rearrange("p n (s h) -> p s n h", h=2)
            for hh in range(2):
                op = tt_(cumf[:, 0, :, :, hh], pairs(cum)[:, :, :, hh], pairs(carry)[:, :, :, hh], ALU.add)
            op.then_inc(gate_dve, 1)
            dve.wait_ge(gate_dve, 7 + NT)
            ts_(cumf[:, 1, :, :, :].rearrange("p s n h -> p (s n h)"), cumf[:, 0, :, :, :].rearrange("p s n h -> p (s n h)"),
                -1.0, None, ALU.mult).then_inc(gate_dve, 1)
            dve.wait_ge(gate_dve, 8 + NT)
            dve.wait_ge(gate_act, 8)

            with dve.Fori(0, STEPS) as i:
                nc.vector.tensor_copy(g_sc[:, :, :], gsc[:, :, bass.ds(i, 1), :].rearrange("p k a n -> p k (a n)")
                                      ).then_inc(head_ready, 1)
                for t in range(2):
                    nc.vector.tensor_copy(qk_tok[:, t, :, :, FD + 1 - t],
                                          cumf[:, t, bass.ds(i, 1), :, :].rearrange("p a n h -> p (a n) h")
                                          ).then_inc(qk_cum, 1)
                nc.vector.memset(state[:, :], 0.0).then_inc(head_ready, 1)

                def proj(m, q):
                    if q < 3 or m not in (GK, GQ, GV):
                        return
                    dve.wait_ge(proj_read, i * STEP_TILES + m + 1)
                    c = (GK, GQ, GV).index(m)
                    dst = (gk, gq, gv)[c]
                    part = (1, 0, 2)[c]
                    for j in range(CONV):
                        tap = conv_taps[:, part, j:j + 1]
                        if j == 0:
                            ts_(dst, g_in[:, 0:S], tap, None, ALU.mult).then_inc(conv_acc, 1)
                        else:
                            dve.wait_ge(conv_acc, i * 9 + 3 * c + j)
                            stt(dst, g_in[:, j:j + S], tap, dst, ALU.mult, ALU.add).then_inc(
                                conv_acc if j < CONV - 1 else conv_done, 1)

                def silu(c, part):
                    dst, t = (gk, gq, gv, gz)[c], silu_scratch[c]
                    if part == 1:
                        dve.wait_ge(silu_act, i * 16 + c * 4 + 3)
                        stt(t, dst, 0.0, t, ALU.min, ALU.subtract).then_inc(silu_arg, 1)
                    elif part == 2:
                        dve.wait_ge(silu_act, i * 16 + c * 4 + 4)
                        tt_(dst, dst, t, ALU.mult).then_inc(silu_done, 1)

                def tok16(t):
                    return t.rearrange("p n h d -> p (n h) d")

                def fox_in(t):
                    if t == 2:
                        return
                    n = i * 2 + t + 1
                    dve.wait_ge(f_sq, n)
                    nc.vector.tensor_reduce(f_ss[:, :], tok16(o_tok[:, :, :, :]), AX.X, ALU.add).then_inc(f_ssd, 1)
                    dve.wait_ge(f_rd, n)
                    dst = tok16(qk_tok[:, t, :, :, 0:FD])
                    tt_(dst, bank2(4).rearrange("p (n d) -> p n d", d=FD), bc(f_r[:, :], FD), ALU.mult).then_inc(qk_scaled, 1)
                    if t == 0:
                        dve.wait_ge(qk_scaled, n)
                        tt_(dst, dst, gain_q[:, :].unsqueeze(1).to_broadcast([P, NT * 2, FD]), ALU.mult
                            ).then_inc(q_gained, 1)

                def scores(u):
                    width = P * (UNITS[u][1] + 1)
                    dve.wait_ge(scores_ready, i * 16 + u + 1)
                    nc.vector.tensor_reduce(nmax[:, u % 2:u % 2 + 1], bank2(2 * (u % 2))[:, 0:width], AX.X, ALU.max,
                                            negate=True).then_inc(max_ready, 1)

                def turn(u):
                    for g in range(UNITS[u][1] // 4 + 1):
                        if TURNS[u, g] % 2:
                            copy_turned(dve, nc.vector.tensor_copy, i, u, g)

                def values(u):
                    hh, n = UNITS[u]
                    src = ps[:, 2 * (u % 2), :]
                    dve.wait_ge(o_done, ONE + i * 16 + u + 1)
                    nc.vector.reciprocal(rl[:, u % 2:u % 2 + 1], src[:, FD:FD + 1]).then_inc(rl_ready, 1)
                    dve.wait_ge(rl_ready, i * 16 + u + 1)
                    ts_(o_tok[:, n, hh, :], src[:, 0:FD], rl[:, u % 2:u % 2 + 1], None, ALU.mult).then_inc(o_read, 1)

                def fox_norm():
                    o16 = tok16(o_tok[:, :, :, :])
                    dve.wait_ge(o_sq, i + 1)
                    nc.vector.tensor_reduce(f_ss[:, :], f_in[:, :].rearrange("p (n d) -> p n d", d=FD), AX.X, ALU.add
                                            ).then_inc(o_ss, 1)
                    dve.wait_ge(o_r, i + 1)
                    tt_(o16, o16, bc(f_r[:, :], FD), ALU.mult).then_inc(o_scaled, 1)
                    dve.wait_ge(o_scaled, i + 1)
                    tt_(o16, o16, vec[:, V_FO:V_FO + FD].unsqueeze(1).to_broadcast([P, NT * 2, FD]), ALU.mult
                        ).then_inc(o_normed, 1)

                def four(ap):
                    return ap.rearrange("p (c n) -> p c n", c=4)

                def per_chunk(kind, h):
                    return bc(g_sc[:, kind, 4 * h:4 * h + 4], P)

                def normed(h, n):
                    dve.wait_ge(g_rd[h], n)
                    tt_(four(n_tok[h]), four(ps[:, 6 + h, :]), bc(g_r[:, h, :], P), ALU.mult).then_inc(g_empty[6 + h], 1)

                def k_in(h):
                    dve.wait_ge(g_sqd[h], i * 2 + 1)
                    nc.vector.tensor_reduce(g_ss[:, h, :], four(n_tok[h]), AX.X, ALU.add).then_inc(g_ssd[h], 1)
                    tt_(four(decay[h]), tri.unsqueeze(1).to_broadcast([P, 4, P]), per_chunk(K_G, h), ALU.mult
                        ).then_inc(g_tri[h], 1)
                    normed(h, i * 2 + 1)
                    dve.wait_ge(g_empty[6 + h], empty(i, ("k_in", h), 6 + h))
                    tt_(four(kb_tok[h]), four(n_tok[h]), per_chunk(K_BETA, h), ALU.mult).then_inc(g_tok[h], 1)
                    tt_(four(kd[h]), four(n_tok[h]), per_chunk(K_EKD, h), ALU.mult).then_inc(g_tok[h], 1)

                def kb_t(h):
                    dve.wait_ge(g_full[6 + h], full(i, ("kb_t", h), 6 + h))
                    tt_(four(kb_tok[h]), four(kb_tok[h]), per_chunk(K_EG, h), ALU.mult).then_inc(g_tok[h], 1)

                def q_in(h):
                    dve.wait_ge(g_sqd[h], i * 2 + 2)
                    nc.vector.tensor_reduce(g_ss[:, h, :], four(qe_tok[h]), AX.X, ALU.add).then_inc(g_ssd[h], 1)
                    normed(h, i * 2 + 2)
                    dve.wait_ge(g_empty[6 + h], empty(i, ("q_in", h), 6 + h))
                    tt_(four(qe_tok[h]), four(n_tok[h]), per_chunk(K_EG, h), ALU.mult).then_inc(g_tok[h], 1)

                def v_in(h):
                    b = 6 + h
                    dve.wait_ge(g_full[b], full(i, ("v_in", h), b))
                    tt_(four(vb[h]), four(ps[:, b, :]), per_chunk(K_BETA, h), ALU.mult).then_inc(g_empty[b], 1)

                def kk(h):
                    b = 6 + h
                    dve.wait_ge(g_full[b], full(i, ("kk", h), b))
                    tt_(kbT[h], ps[:, b, :], decay[h], ALU.mult).then_inc(g_empty[b], 1)
                    dve.wait_ge(g_empty[b], empty(i, ("kk", h), b))
                    tt_(tmT[h], lt[h], cst[:, C_M0:C_M0 + P].unsqueeze(1).to_broadcast([P, 4, P]), ALU.mult
                        ).then_inc(t_init[h], 1)
                    dve.wait_ge(t_init[h], i * 2 + 1)
                    tt_(tmT[h], tmT[h], ident.unsqueeze(1).to_broadcast([P, 4, P]), ALU.add).then_inc(t_init[h], 1)

                def kq(h):
                    b = 6 + h
                    dve.wait_ge(g_full[b], full(i, ("kq", h), b))
                    tt_(intra[h], ps[:, b, :], decay[h], ALU.mult).then_inc(g_empty[b], 1)

                def lt_(h, l):
                    b = 6 + h
                    dve.wait_ge(g_full[b], full(i, ("lt", h, l), b))
                    c0 = C_LV + (l - 1) * (P // 2)
                    tt_(lt_t[h], ps[:, b, 0:4 * (P // 2)].rearrange("p (c n) -> p c n", c=4),
                        cst[:, c0:c0 + P // 2].unsqueeze(1).to_broadcast([P, 4, P // 2]), ALU.mult).then_inc(g_empty[b], 1)

                def tlt(h, l):
                    b = 6 + h
                    dve.wait_ge(g_full[b], full(i, ("tlt", h, l), b))
                    first = evens(tm[h], l)
                    tt_(first, first, blocks(ps[:, b, 0:4 * (P // 2)].rearrange("p (c n) -> p c n", c=4), l),
                        ALU.subtract).then_inc(g_empty[b], 1)

                def u_(h):
                    b = 6 + h
                    dve.wait_ge(g_full[b], full(i, ("u", h), b))
                    nc.vector.tensor_copy(qT[h], ps[:, b, :]).then_inc(g_empty[b], 1)

                def read(h, c):
                    dve.wait_ge(g_full[6], full(i, ("read", h, c), 6))
                    if c == 0:
                        dve.wait_ge(g_empty[6 + h], empty(i, ("u", h), 6 + h))
                    tt_(vnew[:, :], u_tok[h][:, c, :], ps[:, 6, 0:P], ALU.subtract).then_inc(g_empty[6], 1)

                def write(h, c):
                    dve.wait_ge(g_full[6], full(i, ("write", h, c), 6))
                    n = 4 * h + c
                    stt(state[:, :], state[:, :], g_sc[:, K_EGL, n:n + 1], ps[:, 6, 0:P], ALU.mult, ALU.add
                        ).then_inc(g_empty[6], 1)

                def gdn_norm():
                    dve.wait_ge(gn_rms, i + 1)
                    stt(gv, gv, vec[:, V_GON:V_GON + 1], gq, ALU.mult, ALU.mult).then_inc(gn_scaled, 1)
                    dve.wait_ge(gn_scaled, i + 1)
                    tt_(gz, gz, gv, ALU.mult).then_inc(g_out, 1)

                nc.vector.tensor_copy(conv_taps[:, :, :], conv_all[:, :, bass.ds(i, 1), :].rearrange("p t a j -> p t (a j)")
                                      ).then_inc(head_ready, 1)
                dve.wait_ge(head_ready, i * 3 + 3)

                step = {"proj": proj, "silu": silu, "fox_in": fox_in, "scores": scores, "turn": turn, "values": values,
                        "fox_norm": fox_norm, "k_in": k_in, "kb_t": kb_t, "q_in": q_in, "v_in": v_in, "kk": kk, "kq": kq,
                        "lt": lt_, "tlt": tlt, "u": u_, "read": read, "write": write, "gdn_norm": gdn_norm}
                for name, *args in SCHEDULE:
                    if name in step:
                        step[name](*args)
            tail_vector(dve)


_NAMES = ["xt", "memt", "wstream", "wgate", "consts", "vecs"]


def _consts(np):
    r, c = np.arange(P)[:, None], np.arange(P)[None, :]
    parts = [r == c, r <= c, np.ones((P, P)), -1.0 * ((c == r + 1) & (r % 2 == 0)),
             np.where(c > r, NEG, 0.0), np.where(c < r, NEG, 0.0)]
    for l in range(1, LEVELS):
        s = 2 ** l
        col = np.arange(P // 2)
        col = col // s * 2 * s + col % s
        parts.append(r // s == col[None, :] // s + 1)
    return np.concatenate([np.asarray(p, np.float32) for p in parts], axis=1)


def _tiles(np, w):
    k, m = w.shape
    return w.reshape(k // P, P, m // P, P).transpose(2, 1, 0, 3).reshape(m // P, P, -1)


def _columns(np, v):
    return v.reshape(-1, P).T


def kernel(**inputs):
    import numpy as np
    import concourse.bacc as bacc
    from concourse.bass_utils import run_bass_kernel_spmd as run

    a = {k: np.asarray(v) for k, v in inputs.items()}
    w_in = a["w_in"][0]
    fox, gate_f, gdn, gate_ba, z = np.split(
        w_in, np.cumsum([3 * FH * FD, FH, 3 * GH * GD, 2 * GH]).tolist(), axis=1)
    fox_t, gdn_t, z_t = _tiles(np, fox), _tiles(np, gdn), _tiles(np, z)
    stream = []
    for i in range(STEPS):
        stream += [gdn_t[GH + i], gdn_t[i], gdn_t[2 * GH + i], fox_t[i], fox_t[STEPS + i], fox_t[2 * STEPS + i], z_t[i]]
    stream += list(_tiles(np, a["w_out"][0])) + list(_tiles(np, a["w_ckv"][0])) + list(_tiles(np, a["w_cq"][0]))

    def pairs(w):
        t = _tiles(np, w)
        return list(t.reshape(t.shape[0] // 2, 2, P, -1).transpose(0, 2, 1, 3).reshape(t.shape[0] // 2, P, -1))

    stream += pairs(a["w_co"][0])
    w1 = _tiles(np, a["w_mlp1"][0])
    w2 = a["w_mlp2"][0]
    for g in range(FF_GROUPS):
        stream += list(w1[FF_PER * g:FF_PER * (g + 1)]) + pairs(w2[FF_PER * P * g:FF_PER * P * (g + 1)])
    conv = a["gdn_conv_w"][0].reshape(CONV, 3 * GH, P).transpose(2, 1, 0).reshape(P, -1)
    bias = np.concatenate([a["fox_f_bias"][0], np.zeros(GH, np.float32), a["gdn_dt_bias"][0]])
    every = lambda v: np.broadcast_to(v[None, :], (P, v.shape[0]))
    vecs = np.concatenate([_columns(np, a[n][0]) for n in ("norm_mix_g", "norm_xattn_g", "mem_norm_g", "norm_mlp_g")]
                          + [conv] + [_columns(np, a[n][0]) for n in ("gdn_onorm_g", "xattn_qnorm_g", "xattn_knorm_g")]
                          + [every(bias), every(a["gdn_A_log"][0]), every(a["fox_qnorm_g"][0]),
                             every(a["fox_knorm_g"][0]), every(a["fox_onorm_g"][0])], axis=1)
    arrays = {
        "xt": a["x"][0].T.reshape(KT, P, S),
        "memt": a["mem"][0].T.reshape(KT, P, MEM).transpose(1, 0, 2),
        "wstream": np.stack(stream),
        "wgate": np.concatenate([gate_f, gate_ba], axis=1).reshape(KT, P, GATES).transpose(1, 0, 2),
        "consts": _consts(np),
        "vecs": vecs,
    }
    arrays = {k: np.ascontiguousarray(v) for k, v in arrays.items()}
    nc = bacc.Bacc("TRN2", target_bir_lowering=False, num_devices=1)
    args = [nc.dram_tensor(n, arrays[n].shape, F32, kind="ExternalInput").ap() for n in _NAMES]
    out = nc.dram_tensor("out", (KT, P, S), F32, kind="ExternalOutput").ap()
    build_layer(nc, *args, out)
    r = run(nc, [arrays], core_ids=[0])
    return np.ascontiguousarray(r.results[0]["out"].reshape(D, S).T)[None]
```

```python
import math
from contextlib import ExitStack

import concourse.bass as bass
from concourse import mybir

F32 = mybir.dt.float32
F32R = mybir.dt.float32r
BF16 = mybir.dt.bfloat16
ALU = mybir.AluOpType
ACT = mybir.ActivationFunctionType
AX = mybir.AxisListType

P = 128
D = 1024
S = 1024
KT = D // P
NT = S // P
HALF = 512
FH, FD = 8, 64
GH, GD = 4, 128
XH, XD = 4, 128
MEM = 256
MT = MEM // P
DFF = 4 * D
EPS = 1e-6
XS_BANK = (4, 0)
ONE = 1
NEG = -1e30
GATES = FH + 2 * GH
QA = FD + 2
STEPS = GH
CONV = 4
LEVELS = 7

GK, GQ, GV, FQ, FK, FV, GZ = range(7)
STEP_TILES = 7
OUT_TILES, CK_TILES, CV_TILES, CQ_TILES, CO_TILES = KT, XH, XH, XH, KT // 2
FF_GROUPS, FF_PER = 8, 4
W2_TILES = KT // 2
T_MIX = 0
T_OUT = T_MIX + STEPS * STEP_TILES
T_CK = T_OUT + OUT_TILES
T_CV = T_CK + CK_TILES
T_CQ = T_CV + CV_TILES
T_CO = T_CQ + CQ_TILES
T_MLP = T_CO + CO_TILES
TILES = T_MLP + FF_GROUPS * (FF_PER + W2_TILES)
PHASES = [(T_MIX, STEPS, STEP_TILES), (T_OUT, (T_MLP - T_OUT) // 4, 4),
          (T_MLP, FF_GROUPS, FF_PER + W2_TILES)]

MIXED = [k for i in range(STEPS) for k in (i, STEPS + i)]
MIXED_EARLY = KT - 2

C_ID, C_TRI, C_ONE, C_M0, C_NEGF, C_NEGG = (P * n for n in range(6))
C_LV = 6 * P
C_END = C_LV + (LEVELS - 1) * (P // 2)
V_MIX, V_XAT, V_MEM, V_MLP = 0, 8, 16, 24
V_CONV = 32
V_GON, V_XQ, V_XK = 80, 81, 82
V_BIAS = 83
V_ALOG = 99
V_FQ, V_FK, V_FO = 103, 167, 231
V_END = 295

K_G, K_NGC, K_EG, K_EGL, K_EKD, K_BETA = range(6)

LEAD, SPACE_PREP, SPACE_LEVEL, SPACE_SCAN = 2.5, 1.6, 1.1, 1.7
SPACES = {("k_in", 0): 0.0}
UNITS = [(0, n) for n in range(NT)] + [(1, n) for n in reversed(range(NT))]
PREPARE = ["k_in", "k_t", "kb_t", "decay", "q_in", "q_t", "qe_t", "kk", "kq", "v_in", "t_first"]


def mixer_schedule():
    tile = 4 * 2.6
    main = []

    def project(m, between={}):
        before = {GQ: 0, GV: 1, FQ: 2}.get(m)
        for q in range(4):
            main.append((("proj", m, q), tile / 4))
            if before is not None and q < 3:
                main.extend((("silu", before, part), 0.0) for part in ((0, 1, 2), (3, 4), (5,))[q])
            main.extend((o, 1.0) for o in between.get(q, ()))

    for m in (GK, GQ, GV, FQ):
        project(m)
    project(FK, {0: [("fox_in", 0)], 3: [("fox_out", 0, 0)]})
    project(FV, {0: [("fox_out", 0, 1)], 1: [("fox_in", 1)]})
    project(GZ, {0: [("fox_out", 1, 0)], 1: [("fox_out", 1, 1)], 2: [("fox_in", 2)]})
    main += [(("scores", 0), 0.5)]
    for u in range(2 * NT):
        n = UNITS[u][1] + 1
        main += [(("turn", u), 0.11 * n)]
        if u + 1 < 2 * NT:
            main.append((("scores", u + 1), 0.1 + 0.43 * (UNITS[u + 1][1] + 1)))
        main += [(("values", u), 0.22 * n)]
        if 1 <= u < 7:
            main.append((("silu", 3, u - 1), 0.0))
    main += [(("fox_norm",), 1.0)]
    prep, scan = [], []
    for name in PREPARE:
        prep += [(name, h) for h in range(2)]
    for l in range(1, LEVELS):
        for name in ("lt", "tlt", "tt"):
            prep += [(name, h, l) for h in range(2)]
    for name in ("w", "u"):
        prep += [(name, h) for h in range(2)]
    for h in range(2):
        for c in range(4):
            scan += [("read", h, c), ("write", h, c)]
    fill = [(p, SPACES.get(p, SPACE_PREP if p[0] in PREPARE else SPACE_LEVEL)) for p in prep]
    fill += [(p, SPACE_SCAN) for p in scan]
    needs = {"k_in": ("silu", 0, 5), "q_in": ("silu", 1, 5), "v_in": ("silu", 2, 5)}
    out, now, due, at = [], 0.0, 2 * tile + LEAD, 0
    for piece, cost in main:
        if piece[0] == "values" and at < len(fill) and out[-1][0] not in ("read", "write"):
            out.append(fill[at][0])
            due += fill[at][1]
            at += 1
        out.append(piece)
        now += cost
        while (at < len(fill) and now >= due and needs.get(fill[at][0][0]) in [None] + out
               and not (fill[at][0][0] in ("read", "write") and out[-1][0] in ("read", "write"))):
            out.append(fill[at][0])
            due += fill[at][1]
            at += 1
    out += [p for p, _ in fill[at:]]
    return out + [("gdn_norm",), ("fox_store",), ("gdn_store",)]


SCHEDULE = mixer_schedule()
TURNS = {}
for _u in range(2 * NT):
    for _g in range(UNITS[_u][1] // 4 + 1):
        TURNS[_u, _g] = len(TURNS)
N_TURNS = len(TURNS)


def build_layer(nc, xt, memt, wstream, wgate, consts, vecs, out):
    with ExitStack() as ctx:
        def sb(name, shape, dt=F32, c=ctx):
            return c.enter_context(nc.sbuf_tensor(name, shape, dt))

        def sem(name):
            return ctx.enter_context(nc.semaphore(name))

        raw = sb("raw", [P, 2, KT * P])
        w_hi = sb("w_hi", [P, 2, KT, P], F32R)
        w_lo = sb("w_lo", [P, 2, KT, P], F32R)
        h_hi = sb("h_hi", [P, KT, S], F32R)
        h_lo = sb("h_lo", [P, KT, S], F32R)
        x = sb("x", [P, KT, S])
        cst = sb("cst", [P, C_END])
        vec = sb("vec", [P, V_END])
        ident_b = sb("ident_b", [P, P], BF16)
        neg_b = sb("neg_b", [P, 2, P], BF16)
        ident, tri, ones = (cst[:, c:c + P] for c in (C_ID, C_TRI, C_ONE))
        eps_t = sb("eps_t", [P, 1])
        qbias = sb("qbias", [P, 2])

        mix = ExitStack()
        msb = lambda name, shape, dt=F32: sb(name, shape, dt, mix)
        xf = x[:, :, :].rearrange("p k s -> p (k s)")
        gk, gq, gv, gz = (xf[:, S * n:S * (n + 1)] for n in range(4))
        halves = lambda ap: [ap[:, HALF * h:HALF * (h + 1)] for h in range(2)]
        chunks = lambda aps: [ap.rearrange("p (c n) -> p c n", n=P) for ap in aps]
        kd, qeT, vb = halves(gk), halves(gq), halves(gv)
        g_in = msb("g_in", [P, CONV - 1 + S])
        silu_scratch = [gz, gz, gz, g_in[:, CONV - 1:]]
        kT, kbT, qT, decay = (halves(xf[:, S * n:S * (n + 1)]) for n in range(4, 8))
        intra, wT, u_tok = kT, kbT, chunks(qT)
        lt, tm = chunks(kbT), chunks(qT)
        kb_tok = halves(msb("kb_tok", [P, S]))
        n_tok = halves(msb("n_tok", [P, S]))
        tmT_both = halves(msb("tmT", [P, S]))
        qe_tok, tmT = tmT_both, chunks(tmT_both)
        lt_t = [ap[:, 0:4 * (P // 2)].rearrange("p (c n) -> p c n", c=4) for ap in n_tok]
        state = msb("state", [P, P])
        vnew = msb("vnew", [P, P])
        g_ss = msb("g_ss", [P, 2, 4])
        g_ln = msb("g_ln", [P, 2, 4])
        g_r = msb("g_r", [P, 2, 4])
        g_sc = msb("g_sc", [P, 6, NT])
        f_in = msb("f_in", [P, S])
        qk_tok = msb("qk_tok", [P, 2, NT, 2, QA])
        qkT = msb("qkT", [QA, 2, 2, S])
        v_tok = msb("v_tok", [P, NT, 2, FD + 1])
        probs = msb("probs", [P, 2, S])
        probsT = msb("probsT", [P, 4, HALF])
        o_tok = msb("o_tok", [P, NT, 2, FD])
        f_ss = msb("f_ss", [P, NT * 2])
        f_ln = msb("f_ln", [P, NT * 2])
        f_r = msb("f_r", [P, NT * 2])
        nmax = msb("nmax", [P, 2])
        rl = msb("rl", [P, 2])
        gain_q = msb("gain_q", [P, FD])
        gate_w = msb("gate_w", [P, KT, GATES])
        gate_hi = msb("gate_hi", [P, KT, GATES], F32R)
        gate_lo = msb("gate_lo", [P, KT, GATES], F32R)
        gates_tok = msb("gates_tok", [P, NT, GATES])
        ga = msb("ga", [P, NT, GATES])
        gb = msb("gb", [P, NT, GATES])
        glog = msb("glog", [P, NT, FH + GH])
        cum = msb("cum", [P, NT, FH + GH])
        tot = msb("tot", [P, NT, FH + GH])
        carry = msb("carry", [P, NT, FH])
        cumf = msb("cumf", [P, 2, STEPS, NT, 2])
        a_exp = msb("a_exp", [P, GH])
        gsc = msb("gsc", [P, 6, GH, NT])
        conv_taps = msb("conv_taps", [P, 3, CONV])
        conv_all = vec[:, V_CONV:V_CONV + 3 * GH * CONV].rearrange("p (t h j) -> p t h j", h=GH, j=CONV)
        mix.close()

        tail = ExitStack()
        tsb = lambda name, shape, dt=F32: sb(name, shape, dt, tail)
        part_hi = tsb("part_hi", [P, FF_PER, S], F32R)
        part_lo = tsb("part_lo", [P, FF_PER, S], F32R)
        rms = tsb("rms", [P, S])
        x_rms = tsb("x_rms", [P, S])
        tmp = tsb("tmp", [P, 2, S])
        kx = tsb("kx", [P, XH, MEM])
        vx = tsb("vx", [P, XH, MT, P])
        vh = tsb("vh", [P, 2, MT, P])
        mx = tsb("mx", [P, KT * MEM])
        kv = tsb("kv", [P, 2, XH * MEM])
        xmax = tsb("xmax", [P, 2, 4])
        xsum = tsb("xsum", [P, 2, 4])
        xr = tsb("xr", [P, 2, 4])
        gain_x = tsb("gain_x", [P, 1])
        tail.close()
        ps = ctx.enter_context(nc.psum_tensor("ps", [P, 8, HALF], F32))
        mixed = nc.dram_tensor("mixed", (KT, P, S), F32, kind="Internal").ap()

        consts_loaded = sem("consts_loaded")
        gatew_loaded = sem("gatew_loaded")
        x_loaded = [sem(f"x_loaded{k}") for k in range(KT)]
        raw_loaded = [sem(f"raw_loaded{s}") for s in range(2)]
        w_rounded = sem("w_rounded")
        w_split = sem("w_split")
        w_used = sem("w_used")
        gatew_rounded = sem("gatew_rounded")
        gatew_split = sem("gatew_split")
        prepared = sem("prepared")
        gained = sem("gained")
        n_sq, n_sum, n_ps, n_ln, n_rms, n_h, n_hi, n_lo = (
            sem(f"norm_{s}") for s in ("sq", "sum", "ps", "ln", "rms", "h", "hi", "lo"))
        gate_ps, gate_rows, gate_turned, gate_dve, gate_act, cum_ps, cum_read = (
            sem(s) for s in ("gate_ps", "gate_rows", "gate_turned", "gate_dve", "gate_act", "cum_ps", "cum_read"))
        proj_read = sem("proj_read")
        conv_acc = sem("conv_acc")
        conv_done = sem("conv_done")
        silu_act = sem("silu_act")
        silu_arg = sem("silu_arg")
        silu_done = sem("silu_done")
        fox_turned = sem("fox_turned")
        f_sq, f_ssd, f_lnd, f_rd, qk_scaled, q_gained, qk_cum, v_copied = (
            sem(s) for s in ("f_sq", "f_ssd", "f_lnd", "f_rd", "qk_scaled", "q_gained", "qk_cum", "v_copied"))
        qkT_turned, qkT_copied = sem("qkT_turned"), sem("qkT_copied")
        scores_ready, max_ready, probs_ready, turned, o_done, rl_ready, o_read = (
            sem(s) for s in ("scores_ready", "max_ready", "probs_ready", "turned", "o_done", "rl_ready", "o_read"))
        probT_by = [sem("probT_act"), sem("probT_dve")]
        o_sq, o_ss, o_ln, o_r, o_scaled, o_normed, o_turned, o_staged = (
            sem(s) for s in ("o_sq", "o_ss", "o_ln", "o_r", "o_scaled", "o_normed", "o_turned", "o_staged"))
        stored_f, stored_g = sem("stored_f"), sem("stored_g")
        g_full = {6: sem("g_full6"), 7: sem("g_full7")}
        g_empty = {6: sem("g_empty6"), 7: sem("g_empty7")}
        head_ready = sem("head_ready")
        g_sqd, g_ssd, g_lnd, g_rd, g_tok, g_tri, t_init = (
            [sem(f"{s}{h}") for h in range(2)] for s in ("g_sqd", "g_ssd", "g_lnd", "g_rd", "g_tok", "g_tri", "t_init"))
        gn_sq, gn_rms, gn_scaled, g_out = (sem(s) for s in ("gn_sq", "gn_rms", "gn_scaled", "g_out"))
        mixed_in = [sem("mixed_in0"), sem("mixed_in1")]
        mixed_hi, mixed_lo = sem("mixed_hi"), sem("mixed_lo")
        tail_read = sem("tail_read")
        mem_loaded = sem("mem_loaded")
        kv_squared, kv_sums, kv_ln, kx_ready, vt_copied, vx_turned, vx_ready, vh_ready = (
            sem(s) for s in ("kv_squared", "kv_sums", "kv_ln", "kx_ready", "vt_copied", "vx_turned", "vx_ready",
                             "vh_ready"))
        xq_scaled = sem("xq_scaled")
        xq_squared, xq_sums, xq_ln, xq_rms, xq_ready, xs_ready, xmax_ready, xe_ready, xr_ready = (
            sem(s) for s in ("xq_squared", "xq_sums", "xq_ln", "xq_rms", "xq_ready", "xs_ready", "xmax_ready",
                             "xe_ready", "xr_ready"))
        xp_ready, xp_turned, xpT_act, xpT_dve, xo_done, xo_hi, xo_lo, co_even, w2_even = (
            sem(s) for s in ("xp_ready", "xp_turned", "xpT_act", "xpT_dve", "xo_done", "xo_hi", "xo_lo", "co_even",
                             "w2_even"))
        ff_relu, ff_sq, ff_hi, ff_lo = (sem(s) for s in ("ff_relu", "ff_sq", "ff_hi", "ff_lo"))
        ff_used = sem("ff_used")
        stored = sem("stored")

        use = {}
        count = {6: 0, 7: 0}
        for piece in SCHEDULE:
            if piece[0] in PREPARE + ["lt", "tlt", "tt", "w", "u"]:
                banks = [6 + piece[1]]
            else:
                banks = {"read": [6, 7], "write": [6], "gdn_norm": [6, 7]}.get(piece[0], [])
            for b in banks:
                use[piece, b] = count[b]
                count[b] += 1
        for h in range(2):
            for c in range(4):
                use[("write", h, c), 7] = use[("read", h, c), 7]

        def full(i, piece, b):
            return i * count[b] + use[piece, b] + 1

        def empty(i, piece, b):
            return ONE + i * count[b] + use[piece, b] + 1

        def free(i, piece, b):
            return ONE + i * count[b] + use[piece, b]

        def bc(ap, n):
            return ap.unsqueeze(2).to_broadcast([P, ap.shape[1], n])

        def bank2(b):
            return ps[:, b:b + 2, :].rearrange("p b n -> p (b n)")

        def flat(ap):
            return ap.rearrange("p a b -> p (a b)")

        def evens(t, l):
            return t.rearrange("p c (n two s) -> p (c n) two s", two=2, s=2 ** l)[:, :, 0, :]

        def blocks(t, l):
            return t.rearrange("p c (n s) -> p (c n) s", s=2 ** l)

        def stream_slot(phase, m):
            return (m + (phase > 0)) % 2

        def loads(phase, it, m):
            slot = stream_slot(phase, m)
            if phase == 0:
                return (4 - slot) * it + m // 2 + 1
            base = (4 - slot) * STEPS + (0 if phase == 1 else (T_MLP - T_OUT) // 2)
            return base + PHASES[phase][2] // 2 * it + m // 2 + 1


        def copy_turned(eng, copy, i, u, g):
            c = TURNS[u, g]
            width = P * (min(4 * g + 4, UNITS[u][1] + 1) - 4 * g)
            eng.wait_ge(turned, i * N_TURNS + c + 1)
            before = next((v for (v, w), d in TURNS.items() if d == c - 4), -1)
            eng.wait_ge(o_done, ONE + i * 16 + before + 1)
            copy(probsT[:, c % 4, 0:width], ps[:, 4 + c % 2, 0:width]).then_inc(probT_by[c % 2], 1)

        def norm_act(act, q, n, src, src_ready, gain, hi, lo, acc, scratch, bank):
            for k in range(KT):
                src_ready(act, k)
                if k >= 3:
                    act.wait_ge(n_sum, 7 * q + k - 2)
                nc.scalar.activation(scratch(k) if k else acc, src(k), ACT.Square).then_inc(n_sq, 1)
            act.wait_ge(n_ps, q + 1)
            for b in range(0, n, HALF):
                w = min(HALF, n - b)
                op = nc.scalar.activation(acc[:, b:b + w], ps[:, bank + b // HALF, 0:w], ACT.Ln, bias=eps_t[:, :],
                                          scale=1.0 / D)
                op.then_inc(n_ln, 1)
            act.wait_ge(n_ln, (0, 2, 3, 5, 7)[q + 1])
            nc.scalar.activation(acc, acc, ACT.Exp, scale=-0.5).then_inc(n_rms, 1)
            for k in range(KT):
                act.wait_ge(n_h, KT * q + k + 1)
                nc.scalar.copy(hi(k), scratch(k)).then_inc(n_hi, 1)

        def norm_add(dve, q, n, src, src_ready, gain, hi, lo, acc, scratch, bank):
            for k in range(1, KT):
                dve.wait_ge(n_sq, KT * q + k + 1)
                dve.wait_ge(n_sum, 7 * q + k - 1)
                nc.vector.tensor_tensor(acc, acc, scratch(k), ALU.add).then_inc(n_sum, 1)

        def norm_apply(dve, q, n, src, src_ready, gain, hi, lo, acc, scratch, bank):
            dve.wait_ge(n_rms, q + 1)
            dve.wait_ge(n_sum, 7 * q + 7)
            for k in range(KT + 1):
                if k < KT:
                    if k >= 2:
                        dve.wait_ge(n_lo, KT * q + k - 1)
                    nc.vector.scalar_tensor_tensor(scratch(k), src(k), vec[:, gain + k:gain + k + 1], acc,
                                                   ALU.mult, ALU.mult).then_inc(n_h, 1)
                if k:
                    dve.wait_ge(n_hi, KT * q + k)
                    nc.vector.tensor_tensor(lo(k - 1), scratch(k - 1), hi(k - 1).bitcast(F32), ALU.subtract
                                            ).then_inc(n_lo, 1)

        def norm_pe(pe, q, n, acc, bank):
            pe.wait_ge(n_sum, 7 * q + 7)
            for b in range(0, n, HALF):
                w = min(HALF, n - b)
                op = nc.tensor.matmul(ps[:, bank + b // HALF, 0:w], ones, acc[:, b:b + w], start=True, stop=True)
            op.then_inc(n_ps, 1)

        mix_scratch = probsT[:, :, :].rearrange("p (t a) b -> p t (a b)", t=2)
        norm_mix = (0, S, lambda k: x[:, k, :], lambda eng, k: eng.wait_ge(x_loaded[k], 16), V_MIX,
                    lambda k: h_hi[:, k, :], lambda k: h_lo[:, k, :], probs[:, 0, :],
                    lambda k: mix_scratch[:, k % 2, :], 6)
        mem_x = mx[:, :].rearrange("p (k n) -> p k n", n=MEM)
        hm_hi = part_hi[:, 0:2, :].rearrange("p a (b n) -> p (a b) n", n=MEM)
        hm_lo = part_lo[:, 0:2, :].rearrange("p a (b n) -> p (a b) n", n=MEM)
        norm_mem = (1, MEM, lambda k: mem_x[:, k, :], lambda eng, k: eng.wait_ge(mem_loaded, 16), V_MEM,
                    lambda k: hm_hi[:, k, :], lambda k: hm_lo[:, k, :], kv[:, 0, 0:MEM],
                    lambda k: kv[:, 1, MEM * (k % 2):MEM * (k % 2 + 1)], 4)

        def square_act(act, q, base, acc):
            for k in range(KT):
                act.wait_ge(tail_read, base + k + 1)
                if k >= 3:
                    act.wait_ge(n_sum, 7 * q + k - 2)
                nc.scalar.activation(tmp[:, k % 2, :] if k else acc, x[:, k, :], ACT.Square).then_inc(n_sq, 1)
                if q == 3:
                    gained_act(act, q, k, V_MLP)

        def gained_act(act, q, k, gain):
            nc.scalar.activation(h_hi[:, k, :], x[:, k, :], ACT.Copy, scale=vec[:, gain + k:gain + k + 1]
                                 ).then_inc(n_hi, 1)

        def gained_dve(dve, q, k, gain):
            dve.wait_ge(n_hi, KT * q + k + 1)
            nc.vector.scalar_tensor_tensor(h_lo[:, k, :], x[:, k, :], vec[:, gain + k:gain + k + 1],
                                           h_hi[:, k, :].bitcast(F32), ALU.mult, ALU.subtract).then_inc(n_lo, 1)

        def sum_dve(dve, q, k, acc):
            if k:
                dve.wait_ge(n_sq, KT * q + k + 1)
                dve.wait_ge(n_sum, 7 * q + k - 1)
                nc.vector.tensor_tensor(acc, acc, tmp[:, k % 2, :], ALU.add).then_inc(n_sum, 1)

        def factor_act(act, q, acc):
            act.wait_ge(n_ps, q + 1)
            for b in range(2):
                nc.scalar.activation(acc[:, HALF * b:HALF * (b + 1)], ps[:, 6 + b, :], ACT.Ln, bias=eps_t[:, :],
                                     scale=1.0 / D).then_inc(n_ln, 1)
            act.wait_ge(n_ln, (0, 2, 3, 5, 7)[q + 1])
            nc.scalar.activation(acc, acc, ACT.Exp, scale=-0.5).then_inc(n_rms, 1)

        xp = [t.rearrange("p (t n) -> p t n", n=MEM) for t in (mx[:, 0:4 * MEM], kv[:, 0, :])]
        xpT = mx[:, 4 * MEM:].rearrange("p (t n) -> p t n", n=HALF)

        def tail_tensor(pe, split_product, gdn_norm, fox_store):
            mm = nc.tensor.matmul

            def product(slot, w0, kts, pair, hi, lo, n=S, before=None):
                for b in range(0, n, HALF):
                    for j, k in enumerate(kts):
                        if before and b == 0:
                            before(k)
                        cols = slice(b, min(b + HALF, n))
                        op = split_product(ps[:, 2 * pair + b // HALF, 0:min(HALF, n)], slot, (k,),
                                           lambda k: hi[:, k, cols], lambda k: lo[:, k, cols], n,
                                           j == 0, j == len(kts) - 1, w0=w0 + j)
                return op

            def out_part(j, places, mixed_wait):
                for b in range(0, S, HALF):
                    cols = slice(b, b + HALF)
                    for n in places:
                        if mixed_wait and b == 0:
                            pe.wait_ge(mixed_lo, n + 1)
                        op = split_product(ps[:, 2 * j + b // HALF, :], stream_slot(1, j), (MIXED[n],),
                                           lambda k: h_hi[:, k, cols], lambda k: h_lo[:, k, cols], HALF,
                                           n == 0, n == KT - 1, w0=MIXED[n])
                return op

            early, late = range(MIXED_EARLY), range(MIXED_EARLY, KT)
            pe.wait_ge(o_read, ONE + 16 * STEPS)
            pe.wait_ge(w_split, ONE + T_OUT + 1)
            out_part(0, early, True)
            gdn_norm(STEPS - 1)
            fox_store(STEPS - 1)
            pe.wait_ge(w_split, ONE + T_OUT + 2)
            out_part(1, early, False)
            out_part(0, late, True).then_inc(w_used, 1)
            out_part(1, late, False).then_inc(w_used, 1)
            for j in range(2, 4):
                pe.wait_ge(w_split, ONE + T_OUT + j + 1)
                pe.wait_ge(tail_read, j + 1)
                if j == 2:
                    norm_pe(pe, 1, MEM, kv[:, 0, 0:MEM], 4)
                    pe.wait_ge(n_ln, 3)
                out_part(j, range(KT), False).then_inc(w_used, 1)
            for j in range(4):
                pe.wait_ge(w_split, ONE + 4 + T_OUT + j + 1)
                pe.wait_ge(tail_read, 4 + j + 1)
                out_part(j, range(KT), False).then_inc(w_used, 1)
            pe.wait_ge(tail_read, 4 + OUT_TILES - 3)

            def mem_part(t0, bank, hd, before=None):
                pe.wait_ge(w_split, ONE + t0 + hd + 1)
                for k in range(KT):
                    if before:
                        before(k)
                    op = split_product(ps[:, bank + hd // 2, MEM * (hd % 2):MEM * (hd % 2 + 1)], stream_slot(1, hd), (k,),
                                       lambda k: hm_hi[:, k, :], lambda k: hm_lo[:, k, :], MEM, k == 0, k == KT - 1,
                                       w0=k)
                op.then_inc(w_used, 1)

            for hd in range(XH):
                mem_part(T_CK, 0, hd, (lambda k: pe.wait_ge(n_lo, KT + k + 1)) if hd == 0 else None)
                if hd == 0:
                    pe.wait_ge(tail_read, 4 + OUT_TILES)
                    norm_pe(pe, 2, S, x_rms[:, :], 6)
            for hd in range(XH):
                mem_part(T_CV, 4, hd)
                if hd == 1:
                    pe.wait_ge(kv_squared, 1)
                    for b in range(2):
                        mm(ps[:, 2 + b, :], ones, kv[:, 0, HALF * b:HALF * (b + 1)], start=True, stop=True
                           ).then_inc(kv_sums, 1)
            pe.wait_ge(vt_copied, 1)
            for hd in range(XH):
                for mt in range(MT):
                    n = hd * MT + mt
                    op = nc.tensor.transpose(ps[:, 4 + n // 4, P * (n % 4):P * (n % 4 + 1)],
                                             kv[:, 1, MEM * hd + P * mt:MEM * hd + P * (mt + 1)], ident)
            op.then_inc(vx_turned, 1)
            pe.wait_ge(kx_ready, 1)
            pe.wait_ge(n_ln, 5)
            with pe.Fori(0, XH // 2) as it:
                def queries(j):
                    pe.wait_ge(w_split, ONE + it * 2 + T_CQ + j + 1)
                    if j:
                        pe.wait_ge(xo_lo, ONE + it * 4)
                    else:
                        pe.wait_ge(xp_ready, ONE + it * 4)
                    for b in range(2):
                        cols = slice(HALF * b, HALF * (b + 1))
                        for k in range(KT):
                            if j == 0 and b == 0:
                                pe.wait_ge(n_lo, 2 * KT + k + 1)
                            op = split_product(ps[:, 2 * j + b, :], stream_slot(1, j), (k,), lambda k: h_hi[:, k, cols],
                                               lambda k: h_lo[:, k, cols], S, k == 0, k == KT - 1, w0=k)
                        if j == 1 and b == 0:
                            sums(0)
                    op.then_inc(w_used, 1)

                def sums(j):
                    pe.wait_ge(xq_squared, it * 2 + j + 1)
                    if j:
                        pe.wait_ge(xq_ln, it * 4 + 2)
                    else:
                        pe.wait_ge(xpT_act, ONE + it * 4)
                        pe.wait_ge(xpT_dve, ONE + it * 4)
                    for b in range(2):
                        mm(ps[:, 6 + b, :], ones, tmp[:, j, HALF * b:HALF * (b + 1)], start=True, stop=True
                           ).then_inc(xq_sums, 1)

                def scores(u):
                    j, g = divmod(u, 2)
                    pe.wait_ge(xq_ready, ONE + it * 2 + j + 1)
                    if u >= 2:
                        pe.wait_ge(xe_ready, it * 4 + u - 1)
                    for t in range(4):
                        q0 = HALF * g + P * t
                        op = mm(ps[:, XS_BANK[u % 2] + t // 2, MEM * (t % 2):MEM * (t % 2 + 1)], tmp[:, j, q0:q0 + P],
                                kx[:, bass.ds(it * 2 + j, 1), :].rearrange("p a n -> p (a n)"), start=True, stop=True)
                    op.then_inc(xs_ready, 1)

                def turn(u):
                    pe.wait_ge(xp_ready, ONE + it * 4 + u + 1)
                    if u == 0:
                        pe.wait_ge(xq_ln, it * 4 + 4)
                    pe.wait_ge(xpT_act, ONE + it * 4 + u)
                    pe.wait_ge(xpT_dve, ONE + it * 4 + u)
                    for mt in range(MT):
                        for t in range(4):
                            op = nc.tensor.transpose(ps[:, 6 + mt, P * t:P * (t + 1)],
                                                     xp[u % 2][:, t, P * mt:P * (mt + 1)], ident)
                        op.then_inc(xp_turned, 1)

                def outputs(u):
                    j = u // 2
                    pe.wait_ge(vh_ready, it * 2 + j + 1)
                    if u == 0:
                        pe.wait_ge(xq_ready, ONE + it * 2 + 2)
                    elif u >= 2:
                        pe.wait_ge(xo_lo, ONE + it * 4 + u - 1)
                    pe.wait_ge(xpT_act, ONE + it * 4 + u + 1)
                    pe.wait_ge(xpT_dve, ONE + it * 4 + u + 1)
                    for mt in range(MT):
                        op = mm(ps[:, 2 + u % 2, :], vh[:, j, mt, :], xpT[:, mt, :], start=(mt == 0), stop=(mt == MT - 1))
                    op.then_inc(xo_done, 1)

                queries(0)
                queries(1)
                scores(0)
                sums(1)
                scores(1)
                for u in range(4):
                    turn(u)
                    if u < 2:
                        scores(u + 2)
                    outputs(u)
            pe.wait_ge(xo_lo, ONE + 2 * XH)
            with pe.Fori(0, CO_TILES // 2) as it:
                for j in range(4):
                    if j % 2 == 0:
                        pe.wait_ge(w_split, ONE + it * 2 + T_CO + j // 2 + 1)
                    pe.wait_ge(tail_read, it * 4 + 9 + j)
                    op = product(stream_slot(1, j // 2), 4 * (j % 2), range(XH), j, part_hi, part_lo)
                    op.then_inc(w_used if j % 2 else co_even, 1)
            def mlp_group(it, first):
                for j in range(FF_PER):
                    pe.wait_ge(w_split, ONE + it * 8 + T_MLP + j + 1)
                    pe.wait_ge(tail_read, it * 8 + 17 + j)
                    if first and j == 3:
                        pe.wait_ge(n_ln, 7)
                    product(stream_slot(2, j), 0, range(KT), j, h_hi, h_lo,
                            before=(lambda k: pe.wait_ge(n_lo, 3 * KT + k + 1)) if first and j == 0 else None
                            ).then_inc(w_used, 1)
                    if first and j == 0:
                        pe.wait_ge(tail_read, 12 + KT)
                        norm_pe(pe, 3, S, rms[:, :], 6)

                def share(j, places):
                    for b in range(0, S, HALF):
                        cols = slice(b, b + HALF)
                        for k in places:
                            if j == 0 and b == 0:
                                pe.wait_ge(ff_lo, ONE + it * 4 + k + 1)
                            op = split_product(ps[:, 2 * (j % 4) + b // HALF, :], stream_slot(2, FF_PER + j // 2), (k,),
                                               lambda k: part_hi[:, k, cols], lambda k: part_lo[:, k, cols], S,
                                               k == 0, k == FF_PER - 1, w0=4 * (j % 2) + k)
                    return op

                pe.wait_ge(w_split, ONE + it * 8 + T_MLP + FF_PER + 1)
                for j in range(2):
                    pe.wait_ge(ff_relu, it * 4 + j + 1)
                    share(j, range(FF_PER - 1))
                share(0, [FF_PER - 1]).then_inc(w2_even, 1)
                share(1, [FF_PER - 1]).then_inc(w_used, 1)
                for j in range(2, KT):
                    if j % 2 == 0:
                        pe.wait_ge(w_split, ONE + it * 8 + T_MLP + FF_PER + j // 2 + 1)
                    if j < 4:
                        pe.wait_ge(ff_relu, it * 4 + j + 1)
                    else:
                        pe.wait_ge(tail_read, it * 8 + 17 + j)
                    share(j, range(FF_PER)).then_inc(w_used if j % 2 else w2_even, 1)

            mlp_group(0, True)
            with pe.Fori(1, FF_GROUPS) as it:
                mlp_group(it, False)

        def tail_scalar(act):
            act.wait_ge(stored_f, ONE + 16 * STEPS)
            act.wait_ge(stored_g, ONE + 16 * STEPS)
            act.wait_ge(mixed_lo, KT)
            act.dma_start(mem_x, memt).then_inc(mem_loaded, 16)
            for k in range(KT):
                act.dma_start(x[:, k, :], xt[k]).then_inc(x_loaded[k], 16)
            norm_act(act, *norm_mem)
            square_act(act, 2, 4, x_rms[:, :])
            factor_act(act, 2, x_rms[:, :])
            for k in range(KT):
                gained_act(act, 2, k, V_XAT)
            act.wait_ge(w_used, ONE + T_CK + XH)
            nc.scalar.activation(kv[:, 0, :], bank2(0), ACT.Square).then_inc(kv_squared, 1)
            act.wait_ge(kv_sums, 2)
            nc.scalar.activation(kv[:, 0, :], bank2(2), ACT.Ln, bias=eps_t[:, :], scale=1.0 / XD).then_inc(kv_ln, 1)
            act.wait_ge(kv_ln, 1)
            nc.scalar.activation(kv[:, 0, :], kv[:, 0, :], ACT.Exp, scale=-0.5).then_inc(kv_ln, 1)
            act.wait_ge(w_used, ONE + T_CV + XH)
            nc.scalar.copy(kv[:, 1, :], bank2(4)).then_inc(vt_copied, 1)
            with act.Fori(0, XH // 2) as it:
                for j in range(2):
                    act.wait_ge(vx_ready, 1)
                    act.wait_ge(xo_done, ONE + it * 4)
                    nc.scalar.copy(vh[:, j, :, :], vx[:, bass.ds(it * 2 + j, 1), :, :].rearrange("p a m n -> p (a m) n")
                                   ).then_inc(vh_ready, 1)
                def squares(j):
                    act.wait_ge(xq_scaled, it * 2 + j + 1)
                    nc.scalar.activation(tmp[:, j, :], bank2(2 * j), ACT.Square).then_inc(xq_squared, 1)

                def factors(j):
                    act.wait_ge(xq_sums, it * 4 + 2 * j + 2)
                    act.wait_ge(xq_ready, ONE + it * 2 + j)
                    for b in range(2):
                        nc.scalar.activation(rms[:, HALF * b:HALF * (b + 1)], ps[:, 6 + b, :], ACT.Ln, bias=eps_t[:, :],
                                             scale=1.0 / XD).then_inc(xq_ln, 1)
                    act.wait_ge(xq_ln, it * 4 + 2 * j + 2)
                    nc.scalar.activation(rms[:, :], rms[:, :], ACT.Exp, scale=-0.5).then_inc(xq_rms, 1)

                def scores(u):
                    act.wait_ge(xmax_ready, it * 4 + u + 1)
                    for t in range(4):
                        op = nc.scalar.activation(xp[u % 2][:, t, :],
                                                  ps[:, XS_BANK[u % 2] + t // 2, MEM * (t % 2):MEM * (t % 2 + 1)],
                                                  ACT.Exp, bias=xmax[:, u % 2, t:t + 1], accum_out=xsum[:, u % 2, t:t + 1])
                    op.then_inc(xe_ready, 1)

                def turn(u):
                    act.wait_ge(xp_turned, it * 8 + u * 2 + 1)
                    act.wait_ge(xo_done, ONE + it * 4 + u)
                    nc.scalar.copy(xpT[:, 0, :], ps[:, 6, :]).then_inc(xpT_act, 1)

                def outputs(u):
                    j, g = divmod(u, 2)
                    act.wait_ge(xo_done, ONE + it * 4 + u + 1)
                    nc.scalar.copy(part_hi[:, bass.ds(it * 2 + j, 1), HALF * g:HALF * (g + 1)
                                           ].rearrange("p a n -> p (a n)"), ps[:, 2 + u % 2, :]).then_inc(xo_hi, 1)

                squares(0)
                factors(0)
                squares(1)
                scores(0)
                factors(1)
                scores(1)
                for u in range(4):
                    turn(u)
                    if u < 2:
                        scores(u + 2)
                    outputs(u)
            square_act(act, 3, 12, rms[:, :])
            factor_act(act, 3, rms[:, :])
            with act.Fori(0, FF_GROUPS) as it:
                for j in range(FF_PER):
                    t = tmp[:, j % 2, :]
                    act.wait_ge(ff_relu, it * 4 + j + 1)
                    nc.scalar.activation(t, t, ACT.Square).then_inc(ff_sq, 1)
                    if j == 0:
                        act.wait_ge(w_used, ONE + it * 8 + T_MLP)
                    act.wait_ge(ff_sq, it * 4 + j + 1)
                    nc.scalar.copy(part_hi[:, j, :], t).then_inc(ff_hi, 1)

        def tail_vector(dve):
            tt_ = nc.vector.tensor_tensor
            dve.wait_ge(stored_f, ONE + 16 * STEPS)
            dve.wait_ge(stored_g, ONE + 16 * STEPS)
            dve.wait_ge(mixed_lo, KT)
            nc.vector.memset(xr[:, :, :], 0.0).then_inc(tail_read, 4)
            norm_add(dve, *norm_mem)
            for k in range(KT + 1):
                if k < KT:
                    if k == 2:
                        norm_apply(dve, *norm_mem)
                    dve.wait_ge(x_loaded[k], 32)
                    dve.wait_ge(w_used, ONE + T_OUT + k + 1)
                    tt_(x[:, k, :], x[:, k, :], bank2(2 * (k % 4)), ALU.add).then_inc(tail_read, 1)
                if k:
                    sum_dve(dve, 2, k - 1, x_rms[:, :])
            for k in range(KT):
                gained_dve(dve, 2, k, V_XAT)
            dve.wait_ge(kv_ln, 2)
            tt_(kx[:, :, :].rearrange("p h n -> p (h n)"), bank2(0), kv[:, 0, :], ALU.mult).then_inc(kx_ready, 1)
            dve.wait_ge(vx_turned, 1)
            nc.vector.tensor_copy(vx[:, :, :, :].rearrange("p h m n -> p (h m n)"), bank2(4)).then_inc(vx_ready, 1)
            dve.wait_ge(n_rms, 3)
            nc.vector.scalar_tensor_tensor(gain_x[:, :], vec[:, V_XQ:V_XQ + 1], XD ** -0.5, vec[:, V_XK:V_XK + 1],
                                           ALU.mult, ALU.mult).then_inc(gained, 1)
            dve.wait_ge(gained, 1)
            with dve.Fori(0, XH // 2) as it:
                def scaled(j):
                    dve.wait_ge(w_used, ONE + it * 2 + T_CQ + j + 1)
                    tt_(bank2(2 * j), bank2(2 * j), x_rms[:, :], ALU.mult).then_inc(xq_scaled, 1)

                def queries(j):
                    dve.wait_ge(xq_rms, it * 2 + j + 1)
                    nc.vector.scalar_tensor_tensor(tmp[:, j, :], bank2(2 * j), gain_x[:, :], rms[:, :], ALU.mult,
                                                   ALU.mult).then_inc(xq_ready, 1)

                def scores(u):
                    dve.wait_ge(xs_ready, it * 4 + u + 1)
                    nc.vector.tensor_reduce(xmax[:, u % 2, :], bank2(XS_BANK[u % 2]).rearrange("p (t n) -> p t n", n=MEM),
                                            AX.X, ALU.max, negate=True).then_inc(xmax_ready, 1)

                def normed(u):
                    dve.wait_ge(xe_ready, it * 4 + u + 1)
                    nc.vector.reciprocal(xr[:, u % 2, :], xsum[:, u % 2, :]).then_inc(xr_ready, 1)
                    dve.wait_ge(xr_ready, it * 4 + u + 1)
                    tt_(xp[u % 2], xp[u % 2], bc(xr[:, u % 2, :], MEM), ALU.mult).then_inc(xp_ready, 1)

                def turn(u):
                    dve.wait_ge(xp_turned, it * 8 + u * 2 + 2)
                    dve.wait_ge(xo_done, ONE + it * 4 + u)
                    nc.vector.tensor_copy(xpT[:, 1, :], ps[:, 7, :]).then_inc(xpT_dve, 1)

                def outputs(u):
                    j, g = divmod(u, 2)
                    dve.wait_ge(xo_hi, it * 4 + u + 1)
                    cols = slice(HALF * g, HALF * (g + 1))
                    at = bass.ds(it * 2 + j, 1)
                    tt_(part_lo[:, at, cols].rearrange("p a n -> p (a n)"), ps[:, 2 + u % 2, :],
                        part_hi[:, at, cols].rearrange("p a n -> p (a n)").bitcast(F32), ALU.subtract
                        ).then_inc(xo_lo, 1)

                scaled(0)
                queries(0)
                scaled(1)
                scores(0)
                normed(0)
                queries(1)
                scores(1)
                for u in range(4):
                    turn(u)
                    if u < 3:
                        normed(u + 1)
                    if u < 2:
                        scores(u + 2)
                    outputs(u)
            for k in range(KT + 1):
                if k < KT:
                    if k % 2:
                        dve.wait_ge(w_used, ONE + T_CO + k // 2 + 1)
                    else:
                        dve.wait_ge(co_even, k // 2 + 1)
                    tt_(x[:, k, :], x[:, k, :], bank2(2 * (k % 4)), ALU.add).then_inc(tail_read, 1)
                if k:
                    sum_dve(dve, 3, k - 1, rms[:, :])
                    gained_dve(dve, 3, k - 1, V_MLP)
            dve.wait_ge(n_rms, 4)
            with dve.Fori(0, FF_GROUPS) as it:
                for j in range(FF_PER):
                    t = tmp[:, j % 2, :]
                    dve.wait_ge(w_used, ONE + it * 8 + T_MLP + j + 1)
                    dve.wait_ge(ff_lo, ONE + it * 4 + max(j - 1, 0))
                    nc.vector.scalar_tensor_tensor(t, bank2(2 * j), 0.0, rms[:, :], ALU.max, ALU.mult).then_inc(ff_relu, 1)
                    dve.wait_ge(ff_hi, it * 4 + j + 1)
                    tt_(part_lo[:, j, :], t, part_hi[:, j, :].bitcast(F32), ALU.subtract).then_inc(ff_lo, 1)
                for j in range(KT):
                    if j % 2:
                        dve.wait_ge(w_used, ONE + it * 8 + T_MLP + FF_PER + j // 2 + 1)
                    else:
                        dve.wait_ge(w2_even, it * 4 + j // 2 + 1)
                    dve.wait_ge(tail_read, it * 8 + 20)
                    tt_(x[:, j, :], x[:, j, :], bank2(2 * (j % 4)), ALU.add).then_inc(tail_read, 1)

        block = ctx.enter_context(nc.Block())

        @block.sync
        def _(sp):
            sp.dma_start(cst[:, :], consts).then_inc(consts_loaded, 16)
            sp.dma_start(vec[:, :], vecs).then_inc(consts_loaded, 16)
            for k in range(KT):
                sp.dma_start(x[:, k, :], xt[k]).then_inc(x_loaded[k], 16)
            sp.dma_start(gate_w[:, :, :], wgate).then_inc(gatew_loaded, 16)
            def load_raw(phase, t, m):
                slot = stream_slot(phase, m)
                sp.dma_start(raw[:, slot, :], wstream[bass.ds(t, 1)].rearrange("a p n -> (a p) n")
                             ).then_inc(raw_loaded[slot], 16)

            def load_mixed(n):
                i = MIXED[n] % STEPS
                sp.wait_ge(stored_f if MIXED[n] < STEPS else stored_g, ONE + 16 * (i + 1))
                sp.dma_start(raw[:, stream_slot(1, n), :], mixed[MIXED[n]]).then_inc(mixed_in[n % 2], 16)

            for phase, (first, turns, per) in enumerate(PHASES):
                if phase == 1:
                    for n in range(MIXED_EARLY):
                        if n < 2:
                            sp.wait_ge(w_split, ONE + T_OUT - 1 + n)
                        else:
                            sp.wait_ge(mixed_lo, n - 1)
                        load_mixed(n)
                    for m in range(2):
                        sp.wait_ge(mixed_lo, MIXED_EARLY - 1 + m)
                        load_raw(1, T_OUT + m, m)
                    for m in range(2, 4):
                        sp.wait_ge(w_split, ONE + T_OUT + m - 1)
                        load_raw(1, T_OUT + m, m)
                with sp.Fori(1 if phase == 1 else 0, turns) as it:
                    for m in range(per):
                        t = it * per + first + m
                        sp.wait_ge(w_split, ONE + (t if phase == 0 and m == 0 else t - 1))
                        load_raw(phase, t, m)
            for k in range(KT):
                sp.wait_ge(tail_read, 12 + KT + (FF_GROUPS - 1) * KT + k + 1)
                sp.dma_start(out[k], x[:, k, :]).then_inc(stored, 16)
            sp.wait_ge(stored, 16 * KT)

        @block.gpsimd
        def _(pool):
            for s in (w_split, w_used, o_read, conv_done, silu_done, o_staged, o_done, g_empty[6], g_empty[7], xq_ready, xo_lo, xp_ready,
                      xo_done, ff_lo, xpT_act, xpT_dve, stored_f, stored_g):
                pool.sem_inc(s, ONE)
            pool.wait_ge(gatew_loaded, 16)
            nc.gpsimd.tensor_scalar(gate_hi[:, :, :], gate_w[:, :, :], 1.0, 1.0, ALU.mult, ALU.mult
                                    ).then_inc(gatew_rounded, 1)
            pool.wait_ge(gatew_rounded, 1)
            nc.gpsimd.tensor_tensor(gate_lo[:, :, :], gate_w[:, :, :], gate_hi[:, :, :].bitcast(F32),
                                    ALU.subtract).then_inc(gatew_split, 1)
            def split_raw(phase, it, t, m):
                slot = stream_slot(phase, m)
                pool.wait_ge(raw_loaded[slot], 16 * loads(phase, it, m))
                pool.nop(nofuse=True)
                nc.gpsimd.tensor_scalar(flat(w_hi[:, slot, :, :]), raw[:, slot, :], 1.0, 1.0,
                                        ALU.mult, ALU.mult).then_inc(w_rounded, 1)
                pool.wait_ge(w_rounded, t + 1)
                nc.gpsimd.tensor_tensor(flat(w_lo[:, slot, :, :]), raw[:, slot, :],
                                        flat(w_hi[:, slot, :, :]).bitcast(F32), ALU.subtract).then_inc(w_split, 1)

            def split_mixed(n, src):
                k = MIXED[n]
                nc.gpsimd.tensor_scalar(h_hi[:, k, :], src, 1.0, 1.0, ALU.mult, ALU.mult).then_inc(mixed_hi, 1)
                pool.wait_ge(mixed_hi, n + 1)
                nc.gpsimd.tensor_tensor(h_lo[:, k, :], src, h_hi[:, k, :].bitcast(F32), ALU.subtract
                                        ).then_inc(mixed_lo, 1)

            for phase, (first, turns, per) in enumerate(PHASES):
                if phase == 1:
                    pool.wait_ge(w_used, ONE + T_OUT)
                    for n in range(MIXED_EARLY):
                        pool.wait_ge(mixed_in[n % 2], 16 * (n // 2 + 1))
                        split_mixed(n, raw[:, stream_slot(1, n), :])
                    for m in range(2):
                        split_raw(1, 0, T_OUT + m, m)
                    pool.wait_ge(o_staged, ONE + STEPS)
                    split_mixed(MIXED_EARLY, f_in[:, :])
                    pool.wait_ge(g_out, STEPS)
                    split_mixed(MIXED_EARLY + 1, gz)
                    for m in range(2, 4):
                        pool.wait_ge(w_used, ONE + T_OUT + m - 1)
                        split_raw(1, 0, T_OUT + m, m)
                with pool.Fori(1 if phase == 1 else 0, turns) as it:
                    for m in range(per):
                        t = it * per + first + m
                        pool.wait_ge(w_used, ONE + (t if phase == 0 and m == 0 else t - 1))
                        split_raw(phase, it, t, m)

        @block.tensor
        def _(pe):
            mm = nc.tensor.matmul

            def split_product(dst, slot, kts, rhs_hi, rhs_lo, n, first, last, w0=0):
                for j, k in enumerate(kts):
                    for a, (w, r) in enumerate(((w_hi, rhs_hi), (w_hi, rhs_lo), (w_lo, rhs_hi))):
                        op = mm(dst, w[:, slot, w0 + j, :], r(k), start=(first and j == 0 and a == 0),
                                stop=(last and j == len(kts) - 1 and a == 2))
                return op

            pe.wait_ge(consts_loaded, 32)
            norm_pe(pe, 0, S, probs[:, 0, :], 6)

            def gate_products(k):
                for b in range(2):
                    cols = slice(HALF * b, HALF * (b + 1))
                    for a, (w, r) in enumerate(((gate_hi, h_hi), (gate_hi, h_lo), (gate_lo, h_hi))):
                        op = mm(ps[0:GATES, 4 + b, :], w[:, k, :], r[:, k, cols],
                                start=(k == 0 and a == 0), stop=(k == KT - 1 and a == 2))
                if k == KT - 1:
                    op.then_inc(gate_ps, 1)

            def gates_turned():
                pe.wait_ge(gate_rows, 1)
                for n in range(NT):
                    op = nc.tensor.transpose(ps[:, 6, GATES * n:GATES * (n + 1)], f_in[0:GATES, P * n:P * (n + 1)],
                                             ident[0:GATES, 0:GATES])
                op.then_inc(gate_turned, 1)

            def gates_summed():
                pe.wait_ge(gate_dve, 5)
                mm(ps[:, 7, 0:NT * (FH + GH)], tri, flat(glog[:, :, :]), start=True, stop=True)
                mm(ps[:, 6, 0:NT * (FH + GH)], ones, flat(glog[:, :, :]), start=True, stop=True).then_inc(cum_ps, 1)
                pe.wait_ge(cum_read, 2)
                pe.wait_ge(prepared, 1)

            def fox_store(i):
                pe.wait_ge(o_normed, i + 1)
                for b in range(2):
                    pe.wait_ge(probT_by[b], (i + 1) * (N_TURNS // 2))
                for n in range(NT):
                    op = nc.tensor.transpose(ps[:, 4 + n // 4, P * (n % 4):P * (n % 4 + 1)],
                                             flat(o_tok[:, n, :, :]), ident)
                op.then_inc(o_turned, 1)

            def gdn_norm(i):
                pe.wait_ge(gn_sq, i + 1)
                for b in range(2):
                    pe.wait_ge(g_empty[6 + b], free(i, ("gdn_norm",), 6 + b))
                    mm(ps[:, 6 + b, :], ones, gk[:, HALF * b:HALF * (b + 1)], start=True, stop=True
                       ).then_inc(g_full[6 + b], 1)

            def mixer_step(i, first):
                def proj(m, q):
                    t = i * STEP_TILES + m
                    if q == 0:
                        pe.wait_ge(w_split, ONE + t + 1)
                        if m < 2:
                            pe.wait_ge(o_read, ONE + i * 16)
                        else:
                            pe.wait_ge(proj_read, i * STEP_TILES + m - 1)
                    if first and m == GK:
                        if q == 0:
                            pe.wait_ge(gatew_split, 1)
                        pe.wait_ge(n_lo, 2 * q + 2)
                        for k in (2 * q, 2 * q + 1):
                            gate_products(k)
                    for b in range(2):
                        cols = slice(HALF * b, HALF * (b + 1))
                        op = split_product(ps[:, 2 * (m % 2) + b, :], m % 2, (2 * q, 2 * q + 1),
                                           lambda k: h_hi[:, k, cols], lambda k: h_lo[:, k, cols], HALF,
                                           q == 0, q == 3, w0=2 * q)
                    if q == 3:
                        op.then_inc(w_used, 1)

                def silu(c, part):
                    pass

                def fox_in(t):
                    pe.wait_ge(proj_read, i * STEP_TILES + FQ + t + 1)
                    if t == 0:
                        pe.wait_ge(o_staged, ONE + i)
                    else:
                        pe.wait_ge(qkT_copied, i * 4 + 2 * t)
                    for n in range(NT):
                        op = nc.tensor.transpose(ps[:, 4 + n // 4, P * (n % 4):P * (n % 4 + 1)],
                                                 f_in[:, P * n:P * (n + 1)], ident)
                    op.then_inc(fox_turned, 1)

                def fox_out(t, hh):
                    if hh:
                        pe.wait_ge(qkT_copied, i * 4 + 2 * t + 1)
                    else:
                        pe.wait_ge(qk_cum, i * 2 + 2)
                        pe.wait_ge(qk_scaled, i * 2 + t + 1)
                        pe.wait_ge(q_gained, i + 1)
                    for n in range(NT):
                        op = nc.tensor.transpose(ps[0:QA, 4 + n // 4, P * (n % 4):P * (n % 4 + 1)],
                                                 qk_tok[:, t, n, hh, :], ident)
                    op.then_inc(qkT_turned, 1)

                def scores(u):
                    hh, n = UNITS[u]
                    b0 = 2 * (u % 2)
                    if u == 0:
                        pe.wait_ge(qkT_copied, i * 4 + 4)
                        pe.wait_ge(proj_read, i * STEP_TILES + 7)
                        pe.wait_ge(v_copied, i + 1)
                    if u >= 2:
                        pe.wait_ge(o_read, ONE + i * 16 + u - 1)
                    width = P * (n + 1)
                    for b in range(n // 4 + 1):
                        w = min(HALF, width - HALF * b)
                        mm(ps[:, b0 + b, 0:w], qkT[0:QA, 0, hh, P * n:P * (n + 1)],
                           qkT[0:QA, 1, hh, HALF * b:HALF * b + w], start=True, stop=True)
                    mm(ps[:, b0 + n // 4, w - P:w], ident_b[:, :], neg_b[:, 0, :], start=False, stop=True,
                       skip_group_check=True).then_inc(scores_ready, 1)

                def turn(u):
                    for g in range(UNITS[u][1] // 4 + 1):
                        c = TURNS[u, g]
                        pe.wait_ge(probs_ready, i * N_TURNS + c + 1)
                        if c >= 2:
                            pe.wait_ge(probT_by[c % 2], i * (N_TURNS // 2) + c // 2)
                        for j in range(4 * g, min(4 * g + 4, UNITS[u][1] + 1)):
                            op = nc.tensor.transpose(ps[:, 4 + c % 2, P * (j % 4):P * (j % 4 + 1)],
                                                     probs[:, u % 2, P * j:P * (j + 1)], ident)
                        op.then_inc(turned, 1)

                def values(u):
                    hh, n = UNITS[u]
                    for g in range(n // 4 + 1):
                        c = TURNS[u, g]
                        pe.wait_ge(probT_by[c % 2], i * (N_TURNS // 2) + c // 2 + 1)
                        for j in range(4 * g, min(4 * g + 4, n + 1)):
                            op = mm(ps[:, 2 * (u % 2), 0:FD + 1], probsT[:, c % 4, P * (j % 4):P * (j % 4 + 1)],
                                    v_tok[:, j, hh, :], start=(j == 0), stop=(j == n))
                    op.then_inc(o_done, 1)

                def turn4(piece, b, src):
                    pe.wait_ge(g_empty[b], free(i, piece, b))
                    for c in range(4):
                        op = nc.tensor.transpose(ps[:, b, P * c:P * (c + 1)], src(c), ident)
                    op.then_inc(g_full[b], 1)

                def times4(piece, b, lhs, rhs, n):
                    pe.wait_ge(g_empty[b], free(i, piece, b))
                    for c in range(4):
                        op = mm(ps[:, b, n * c:n * (c + 1)], lhs(c), rhs(c), start=True, stop=True)
                    op.then_inc(g_full[b], 1)

                def chunk(ap):
                    return lambda c: ap[:, P * c:P * (c + 1)]

                def k_in(h):
                    pe.wait_ge(silu_done, ONE + i * 4 + 1)
                    turn4(("k_in", h), 6 + h, chunk(gk[:, HALF * h:HALF * (h + 1)]))

                def k_t(h):
                    pe.wait_ge(g_empty[6 + h], empty(i, ("k_in", h), 6 + h))
                    turn4(("k_t", h), 6 + h, chunk(n_tok[h]))

                def kb_t(h):
                    pe.wait_ge(g_tok[h], i * 4 + 1)
                    turn4(("kb_t", h), 6 + h, chunk(kb_tok[h]))

                def q_in(h):
                    pe.wait_ge(silu_done, ONE + i * 4 + 2)
                    turn4(("q_in", h), 6 + h, chunk(gq[:, HALF * h:HALF * (h + 1)]))

                def q_t(h):
                    pe.wait_ge(g_empty[6 + h], empty(i, ("q_in", h), 6 + h))
                    turn4(("q_t", h), 6 + h, chunk(n_tok[h]))

                def qe_t(h):
                    pe.wait_ge(g_tok[h], i * 4 + 4)
                    turn4(("qe_t", h), 6 + h, chunk(qe_tok[h]))

                def v_in(h):
                    pe.wait_ge(silu_done, ONE + i * 4 + 3)
                    turn4(("v_in", h), 6 + h, chunk(gv[:, HALF * h:HALF * (h + 1)]))

                def decay_(h):
                    piece, b = ("decay", h), 6 + h
                    pe.wait_ge(g_empty[b], free(i, piece, b))
                    pe.wait_ge(g_tri[h], i + 1)
                    mm(ps[:, b, :], ones, decay[h], start=True, stop=True)
                    for c in range(4):
                        op = mm(ps[:, b, P * c:P * (c + 1)], ident_b[:, :], neg_b[:, 1, :], start=False,
                                stop=True, skip_group_check=True)
                    op.then_inc(g_full[b], 1)

                def kk(h):
                    times4(("kk", h), 6 + h, chunk(kT[h]), chunk(kbT[h]), P)

                def kq(h):
                    times4(("kq", h), 6 + h, chunk(kT[h]), chunk(qT[h]), P)

                def t_first(h):
                    pe.wait_ge(t_init[h], i * 2 + 2)
                    turn4(("t_first", h), 6 + h, lambda c: tmT[h][:, c, :])

                def lt_(h, l):
                    s = 2 ** l
                    times4(("lt", h, l), 6 + h, lambda c: lt[h][:, c, :],
                           lambda c: tm[h][:, c, :].rearrange("p (n two s) -> p n two s", two=2, s=s)[:, :, 0, :],
                           P // 2)

                def tlt(h, l):
                    times4(("tlt", h, l), 6 + h, lambda c: tmT[h][:, c, :], lambda c: lt_t[h][:, c, :], P // 2)

                def tt(h, l):
                    turn4(("tt", h, l), 6 + h, lambda c: tm[h][:, c, :])

                def w_(h):
                    times4(("w", h), 6 + h, chunk(kb_tok[h]), lambda c: tmT[h][:, c, :], P)

                def u_(h):
                    times4(("u", h), 6 + h, lambda c: tmT[h][:, c, :], chunk(vb[h]), P)

                def read(h, c):
                    piece = ("read", h, c)
                    if c == 0:
                        pe.wait_ge(g_empty[6 + h], empty(i, ("w", h), 6 + h))
                    pe.wait_ge(g_empty[6], free(i, piece, 6))
                    mm(ps[:, 6, 0:P], wT[h][:, P * c:P * (c + 1)], state[:, :], start=True, stop=True
                       ).then_inc(g_full[6], 1)
                    pe.wait_ge(g_empty[7], free(i, piece, 7))
                    mm(ps[:, 7, 0:P], state[:, :], qeT[h][:, P * c:P * (c + 1)], start=True, stop=False)

                def write(h, c):
                    pe.wait_ge(g_empty[6], empty(i, ("read", h, c), 6))
                    mm(ps[:, 6, 0:P], kd[h][:, P * c:P * (c + 1)], vnew[:, :], start=True, stop=True
                       ).then_inc(g_full[6], 1)
                    mm(ps[:, 7, 0:P], vnew[:, :], intra[h][:, P * c:P * (c + 1)], start=False, stop=True
                       ).then_inc(g_full[7], 1)

                step = {"proj": proj, "silu": silu, "fox_in": fox_in, "fox_out": fox_out, "scores": scores, "turn": turn,
                        "values": values, "k_in": k_in,
                        "k_t": k_t, "kb_t": kb_t, "q_in": q_in, "q_t": q_t, "qe_t": qe_t, "v_in": v_in,
                        "decay": decay_, "kk": kk,
                        "kq": kq, "t_first": t_first, "lt": lt_, "tlt": tlt, "tt": tt, "w": w_, "u": u_,
                        "read": read, "write": write}
                for name, *args in SCHEDULE:
                    if name in step:
                        step[name](*args)
                    if first and (name, *args) == ("proj", GK, 3):
                        gates_turned()
                    elif first and (name, *args) == ("proj", GQ, 2):
                        gates_summed()
                    if not first and (name, *args) == ("proj", GK, 1):
                        gdn_norm(i - 1)
                    elif not first and (name, *args) == ("proj", GK, 2):
                        fox_store(i - 1)

            mixer_step(0, True)
            with pe.Fori(1, STEPS) as i:
                mixer_step(i, False)
            tail_tensor(pe, split_product, gdn_norm, fox_store)

        @block.scalar
        def _(act):
            nc.scalar.preload_act_table_set("natural_log_exp_and_others")
            norm_act(act, *norm_mix)

            act.wait_ge(gate_ps, 1)
            nc.scalar.copy(f_in[0:GATES, :], bank2(4)[0:GATES, :]).then_inc(gate_rows, 1)
            act.wait_ge(gate_dve, 1)
            nc.scalar.activation(flat(ga[:, :, :]), flat(gates_tok[:, :, :]), ACT.Abs).then_inc(gate_act, 1)
            act.wait_ge(gate_act, 1)
            nc.scalar.activation(flat(ga[:, :, :]), flat(ga[:, :, :]), ACT.Exp, scale=-1.0).then_inc(gate_act, 1)
            act.wait_ge(gate_act, 2)
            nc.scalar.activation(flat(ga[:, :, :]), flat(ga[:, :, :]), ACT.Ln, bias=1.0).then_inc(gate_act, 1)
            nc.scalar.activation(a_exp[:, :], vec[:, V_ALOG:V_ALOG + GH], ACT.Exp).then_inc(gate_act, 1)
            act.wait_ge(gate_dve, 3)
            nc.scalar.activation(gsc[:, K_BETA, :, :], gb[:, :, FH:FH + GH].rearrange("p n g -> p g n"), ACT.Exp
                                 ).then_inc(gate_act, 1)
            act.wait_ge(gate_dve, 6)
            for kind, src in ((K_EG, cum), (K_EGL, tot), (K_EKD, glog)):
                nc.scalar.activation(gsc[:, kind, :, :], src[:, :, FH:].rearrange("p n g -> p g n"), ACT.Exp
                                     ).then_inc(gate_act, 1)

            with act.Fori(0, STEPS) as i:
                def proj(m, q):
                    if q < 3:
                        return
                    act.wait_ge(w_used, ONE + i * STEP_TILES + m + 1)
                    src = bank2(2 * (m % 2))
                    if m in (GK, GQ, GV):
                        c = (GK, GQ, GV).index(m)
                        act.wait_ge(conv_done, ONE + i * 3 + c)
                        nc.scalar.copy(g_in[:, CONV - 1:], src).then_inc(proj_read, 1)
                    elif m == GZ:
                        act.wait_ge(silu_done, ONE + i * 4 + 3)
                        act.wait_ge(stored_g, ONE + i * 16)
                        nc.scalar.copy(gz, src).then_inc(proj_read, 1)
                    else:
                        if m == FQ:
                            act.wait_ge(stored_f, ONE + i * 16)
                        else:
                            act.wait_ge(fox_turned, i * 3 + m - FQ)
                        nc.scalar.copy(f_in[:, :], src).then_inc(proj_read, 1)

                def silu(c, part):
                    dst, t = (gk, gq, gv, gz)[c], silu_scratch[c]
                    if part == 0:
                        if c < 3:
                            act.wait_ge(conv_done, ONE + i * 3 + c + 1)
                            act.wait_ge(silu_done, ONE + i * 4 + c)
                            act.wait_ge(stored_g, ONE + i * 16)
                        else:
                            act.wait_ge(proj_read, i * STEP_TILES + GZ + 1)
                            act.wait_ge(conv_done, ONE + i * 3 + 3)
                        nc.scalar.activation(t, dst, ACT.Abs).then_inc(silu_act, 1)
                    elif part == 1:
                        act.wait_ge(silu_act, i * 16 + c * 4 + 1)
                        nc.scalar.activation(t, t, ACT.Exp, scale=-1.0).then_inc(silu_act, 1)
                    elif part == 2:
                        act.wait_ge(silu_act, i * 16 + c * 4 + 2)
                        nc.scalar.activation(t, t, ACT.Ln, bias=1.0).then_inc(silu_act, 1)
                    elif part == 4:
                        act.wait_ge(silu_arg, i * 4 + c + 1)
                        nc.scalar.activation(t, t, ACT.Exp).then_inc(silu_act, 1)

                def rsqrt16(scale, done_ss, done_ln, done_r, n):
                    act.wait_ge(done_ss, n)
                    nc.scalar.activation(f_ln[:, :], f_ss[:, :], ACT.Ln, bias=eps_t[:, :], scale=scale).then_inc(done_ln, 1)
                    act.wait_ge(done_ln, n)
                    nc.scalar.activation(f_r[:, :], f_ln[:, :], ACT.Exp, scale=-0.5).then_inc(done_r, 1)

                def fox_in(t):
                    act.wait_ge(fox_turned, i * 3 + t + 1)
                    if t == 2:
                        nc.scalar.copy(v_tok[:, :, :, 0:FD], bank2(4).rearrange("p (n h d) -> p n h d", h=2, d=FD)
                                       ).then_inc(v_copied, 1)
                        return
                    if t == 1:
                        act.wait_ge(f_ssd, i * 2 + 1)
                    nc.scalar.activation(o_tok[:, :, :, :].rearrange("p n h d -> p (n h d)"), bank2(4), ACT.Square
                                         ).then_inc(f_sq, 1)
                    rsqrt16(1.0 / FD, f_ssd, f_lnd, f_rd, i * 2 + t + 1)

                def fox_out(t, hh):
                    act.wait_ge(qkT_turned, i * 4 + 2 * t + hh + 1)
                    nc.scalar.copy(qkT[:, t, hh, :], bank2(4)[0:QA, :]).then_inc(qkT_copied, 1)

                def scores(u):
                    pass

                def turn(u):
                    act.wait_ge(max_ready, i * 16 + u + 1)
                    for g in range(UNITS[u][1] // 4 + 1):
                        cols = slice(HALF * g, min(HALF * (g + 1), P * (UNITS[u][1] + 1)))
                        nc.scalar.activation(probs[:, u % 2, cols], bank2(2 * (u % 2))[:, cols], ACT.Exp,
                                             bias=nmax[:, u % 2:u % 2 + 1]).then_inc(probs_ready, 1)
                    for g in range(UNITS[u][1] // 4 + 1):
                        c = TURNS[u, g]
                        if c % 2 == 0:
                            copy_turned(act, nc.scalar.copy, i, u, g)

                def values(u):
                    pass

                def fox_norm():
                    act.wait_ge(o_read, ONE + i * 16 + 16)
                    nc.scalar.activation(f_in[:, :], o_tok[:, :, :, :].rearrange("p n h d -> p (n h d)"), ACT.Square
                                         ).then_inc(o_sq, 1)
                    rsqrt16(1.0 / FD, o_ss, o_ln, o_r, i + 1)

                def fox_store():
                    act.wait_ge(o_turned, i + 1)
                    nc.scalar.copy(f_in[:, :], bank2(4)).then_inc(o_staged, 1)
                    act.wait_ge(o_staged, ONE + i + 1)
                    act.dma_start(mixed[bass.ds(i, 1)].rearrange("a p n -> (a p) n"), f_in[:, :]).then_inc(stored_f, 16)

                def rsqrt4(h, n, bias):
                    act.wait_ge(g_ssd[h], n)
                    nc.scalar.activation(g_ln[:, h, :], g_ss[:, h, :], ACT.Ln, bias=eps_t[:, :]).then_inc(g_lnd[h], 1)
                    act.wait_ge(g_lnd[h], n)
                    nc.scalar.activation(g_r[:, h, :], g_ln[:, h, :], ACT.Exp, scale=-0.5, bias=bias).then_inc(g_rd[h], 1)

                def k_in(h):
                    act.wait_ge(g_full[6 + h], full(i, ("k_in", h), 6 + h))
                    nc.scalar.activation(n_tok[h], ps[:, 6 + h, :], ACT.Square).then_inc(g_sqd[h], 1)
                    rsqrt4(h, i * 2 + 1, 0.0)

                def q_in(h):
                    act.wait_ge(g_full[6 + h], full(i, ("q_in", h), 6 + h))
                    nc.scalar.activation(qe_tok[h], ps[:, 6 + h, :], ACT.Square).then_inc(g_sqd[h], 1)
                    rsqrt4(h, i * 2 + 2, qbias[:, 0:1])

                def copy_out(piece, b, dst):
                    act.wait_ge(g_full[b], full(i, piece, b))
                    nc.scalar.copy(dst, ps[:, b, :]).then_inc(g_empty[b], 1)

                def k_t(h):
                    copy_out(("k_t", h), 6 + h, kT[h])

                def kb_t(h):
                    copy_out(("kb_t", h), 6 + h, kbT[h])

                def q_t(h):
                    copy_out(("q_t", h), 6 + h, qT[h])

                def qe_t(h):
                    copy_out(("qe_t", h), 6 + h, qeT[h])

                def decay_(h):
                    b = 6 + h
                    act.wait_ge(g_full[b], full(i, ("decay", h), b))
                    for c in range(4):
                        op = nc.scalar.activation(decay[h][:, P * c:P * (c + 1)], ps[:, b, P * c:P * (c + 1)], ACT.Exp,
                                                  bias=g_sc[:, K_NGC, 4 * h + c:4 * h + c + 1])
                    op.then_inc(g_empty[b], 1)

                def t_first(h):
                    copy_out(("t_first", h), 6 + h, qT[h])

                def tt(h, l):
                    copy_out(("tt", h, l), 6 + h, tmT_both[h])

                def w_(h):
                    copy_out(("w", h), 6 + h, wT[h])

                def write(h, c):
                    act.wait_ge(g_full[7], full(i, ("write", h, c), 7))
                    nc.scalar.copy(gv[:, HALF * h + P * c:HALF * h + P * (c + 1)], ps[:, 7, 0:P]).then_inc(g_empty[7], 1)

                def gdn_norm():
                    act.wait_ge(g_empty[7], free(i, ("gdn_norm",), 7))
                    act.wait_ge(g_empty[6], free(i, ("gdn_norm",), 6))
                    nc.scalar.activation(gk, gv, ACT.Square).then_inc(gn_sq, 1)
                    for b in range(2):
                        act.wait_ge(g_full[6 + b], full(i, ("gdn_norm",), 6 + b))
                        nc.scalar.activation(gq[:, HALF * b:HALF * (b + 1)], ps[:, 6 + b, :], ACT.Ln, bias=eps_t[:, :],
                                             scale=1.0 / GD).then_inc(g_empty[6 + b], 1)
                    for b in range(2):
                        act.wait_ge(g_empty[6 + b], ONE + i * count[6 + b] + count[6 + b])
                    nc.scalar.activation(gq, gq, ACT.Exp, scale=-0.5).then_inc(gn_rms, 1)

                def gdn_store():
                    act.wait_ge(g_out, i + 1)
                    act.dma_start(mixed[bass.ds(i + STEPS, 1)].rearrange("a p n -> (a p) n"), gz).then_inc(stored_g, 16)

                step = {"proj": proj, "silu": silu, "fox_in": fox_in, "fox_out": fox_out, "scores": scores, "turn": turn,
                        "values": values, "fox_norm": fox_norm, "fox_store": fox_store, "k_in": k_in,
                        "k_t": k_t, "kb_t": kb_t, "q_in": q_in, "q_t": q_t, "qe_t": qe_t, "decay": decay_, "t_first": t_first,
                        "tt": tt, "w": w_, "write": write, "gdn_norm": gdn_norm, "gdn_store": gdn_store}
                for name, *args in SCHEDULE:
                    if name in step:
                        step[name](*args)
            tail_scalar(act)

        @block.vector
        def _(dve):
            tt_ = nc.vector.tensor_tensor
            ts_ = nc.vector.tensor_scalar
            stt = nc.vector.scalar_tensor_tensor
            dve.wait_ge(consts_loaded, 32)
            nc.vector.memset(eps_t[:, :], EPS)
            nc.vector.memset(qbias[:, 0:1], -0.5 * math.log(GD))
            nc.vector.memset(qk_tok[:, 0, :, :, FD:FD + 1], 1.0)
            nc.vector.memset(qk_tok[:, 1, :, :, FD + 1:QA], 1.0)
            nc.vector.memset(v_tok[:, :, :, FD:FD + 1], 1.0)
            nc.vector.memset(g_in[:, 0:CONV - 1], 0.0)
            nc.vector.tensor_copy(neg_b[:, 0, :], cst[:, C_NEGF:C_NEGF + P])
            nc.vector.tensor_copy(neg_b[:, 1, :], cst[:, C_NEGG:C_NEGG + P])
            stt(gain_q[:, :], vec[:, V_FQ:V_FQ + FD], FD ** -0.5, vec[:, V_FK:V_FK + FD], ALU.mult, ALU.mult)
            nc.vector.tensor_copy(ident_b[:, :], ident).then_inc(prepared, 1)
            norm_add(dve, *norm_mix)
            norm_apply(dve, *norm_mix)

            dve.wait_ge(gate_turned, 1)
            tt_(gates_tok[:, :, :], ps[:, 6, 0:NT * GATES].rearrange("p (n g) -> p n g", g=GATES),
                vec[:, V_BIAS:V_BIAS + GATES].unsqueeze(1).to_broadcast([P, NT, GATES]), ALU.add).then_inc(gate_dve, 1)
            dve.wait_ge(gate_act, 3)
            dve.wait_ge(gate_dve, 1)
            stt(flat(gb[:, :, :]), flat(gates_tok[:, :, :]), 0.0, flat(ga[:, :, :]), ALU.min, ALU.subtract).then_inc(gate_dve, 1)
            dve.wait_ge(gate_dve, 2)
            nc.vector.tensor_copy(glog[:, :, 0:FH], gb[:, :, 0:FH]).then_inc(gate_dve, 1)
            stt(gates_tok[:, :, FH + GH:], gates_tok[:, :, FH + GH:], 0.0, ga[:, :, FH + GH:], ALU.max, ALU.add
                ).then_inc(gate_dve, 1)
            dve.wait_ge(gate_dve, 4)
            dve.wait_ge(gate_act, 4)
            stt(glog[:, :, FH:], gates_tok[:, :, FH + GH:], -1.0,
                a_exp[:, :].unsqueeze(1).to_broadcast([P, NT, GH]), ALU.mult, ALU.mult).then_inc(gate_dve, 1)
            dve.wait_ge(gate_dve, 5)
            nc.vector.tensor_copy(gsc[:, K_G, :, :], glog[:, :, FH:].rearrange("p n g -> p g n"))
            dve.wait_ge(cum_ps, 1)
            nc.vector.tensor_copy(flat(cum[:, :, :]), ps[:, 7, 0:NT * (FH + GH)]).then_inc(cum_read, 1)
            nc.vector.tensor_copy(flat(tot[:, :, :]), ps[:, 6, 0:NT * (FH + GH)]).then_inc(cum_read, 1)
            dve.wait_ge(cum_read, 2)
            tt_(glog[:, :, FH:], tot[:, :, FH:], cum[:, :, FH:], ALU.subtract).then_inc(gate_dve, 1)
            ts_(gsc[:, K_NGC, :, :], cum[:, :, FH:].rearrange("p n g -> p g n"), -1.0, None, ALU.mult)
            nc.vector.memset(carry[:, 0, :], 0.0).then_inc(gate_dve, 1)
            for n in range(1, NT):
                dve.wait_ge(gate_dve, 6 + n)
                tt_(carry[:, n, :], carry[:, n - 1, :], tot[:, n - 1, 0:FH], ALU.add).then_inc(gate_dve, 1)
            dve.wait_ge(gate_dve, 6 + NT)
            pairs = lambda t: t[:, :, 0:FH].rearrange("p n (s h) -> p s n h", h=2)
            for hh in range(2):
                op = tt_(cumf[:, 0, :, :, hh], pairs(cum)[:, :, :, hh], pairs(carry)[:, :, :, hh], ALU.add)
            op.then_inc(gate_dve, 1)
            dve.wait_ge(gate_dve, 7 + NT)
            ts_(cumf[:, 1, :, :, :].rearrange("p s n h -> p (s n h)"), cumf[:, 0, :, :, :].rearrange("p s n h -> p (s n h)"),
                -1.0, None, ALU.mult).then_inc(gate_dve, 1)
            dve.wait_ge(gate_dve, 8 + NT)
            dve.wait_ge(gate_act, 8)

            with dve.Fori(0, STEPS) as i:
                nc.vector.tensor_copy(g_sc[:, :, :], gsc[:, :, bass.ds(i, 1), :].rearrange("p k a n -> p k (a n)")
                                      ).then_inc(head_ready, 1)
                for t in range(2):
                    nc.vector.tensor_copy(qk_tok[:, t, :, :, FD + 1 - t],
                                          cumf[:, t, bass.ds(i, 1), :, :].rearrange("p a n h -> p (a n) h")
                                          ).then_inc(qk_cum, 1)
                nc.vector.memset(state[:, :], 0.0).then_inc(head_ready, 1)

                def proj(m, q):
                    if q < 3 or m not in (GK, GQ, GV):
                        return
                    dve.wait_ge(proj_read, i * STEP_TILES + m + 1)
                    c = (GK, GQ, GV).index(m)
                    dst = (gk, gq, gv)[c]
                    part = (1, 0, 2)[c]
                    for j in range(CONV):
                        tap = conv_taps[:, part, j:j + 1]
                        if j == 0:
                            ts_(dst, g_in[:, 0:S], tap, None, ALU.mult).then_inc(conv_acc, 1)
                        else:
                            dve.wait_ge(conv_acc, i * 9 + 3 * c + j)
                            stt(dst, g_in[:, j:j + S], tap, dst, ALU.mult, ALU.add).then_inc(
                                conv_acc if j < CONV - 1 else conv_done, 1)

                def silu(c, part):
                    dst, t = (gk, gq, gv, gz)[c], silu_scratch[c]
                    if part == 3:
                        dve.wait_ge(silu_act, i * 16 + c * 4 + 3)
                        stt(t, dst, 0.0, t, ALU.min, ALU.subtract).then_inc(silu_arg, 1)
                    elif part == 5:
                        dve.wait_ge(silu_act, i * 16 + c * 4 + 4)
                        tt_(dst, dst, t, ALU.mult).then_inc(silu_done, 1)

                def tok16(t):
                    return t.rearrange("p n h d -> p (n h) d")

                def fox_in(t):
                    if t == 2:
                        return
                    n = i * 2 + t + 1
                    dve.wait_ge(f_sq, n)
                    nc.vector.tensor_reduce(f_ss[:, :], tok16(o_tok[:, :, :, :]), AX.X, ALU.add).then_inc(f_ssd, 1)
                    dve.wait_ge(f_rd, n)
                    dst = tok16(qk_tok[:, t, :, :, 0:FD])
                    tt_(dst, bank2(4).rearrange("p (n d) -> p n d", d=FD), bc(f_r[:, :], FD), ALU.mult).then_inc(qk_scaled, 1)
                    if t == 0:
                        dve.wait_ge(qk_scaled, n)
                        tt_(dst, dst, gain_q[:, :].unsqueeze(1).to_broadcast([P, NT * 2, FD]), ALU.mult
                            ).then_inc(q_gained, 1)

                def scores(u):
                    width = P * (UNITS[u][1] + 1)
                    dve.wait_ge(scores_ready, i * 16 + u + 1)
                    nc.vector.tensor_reduce(nmax[:, u % 2:u % 2 + 1], bank2(2 * (u % 2))[:, 0:width], AX.X, ALU.max,
                                            negate=True).then_inc(max_ready, 1)

                def turn(u):
                    for g in range(UNITS[u][1] // 4 + 1):
                        if TURNS[u, g] % 2:
                            copy_turned(dve, nc.vector.tensor_copy, i, u, g)

                def values(u):
                    hh, n = UNITS[u]
                    src = ps[:, 2 * (u % 2), :]
                    dve.wait_ge(o_done, ONE + i * 16 + u + 1)
                    nc.vector.reciprocal(rl[:, u % 2:u % 2 + 1], src[:, FD:FD + 1]).then_inc(rl_ready, 1)
                    dve.wait_ge(rl_ready, i * 16 + u + 1)
                    ts_(o_tok[:, n, hh, :], src[:, 0:FD], rl[:, u % 2:u % 2 + 1], None, ALU.mult).then_inc(o_read, 1)

                def fox_norm():
                    o16 = tok16(o_tok[:, :, :, :])
                    dve.wait_ge(o_sq, i + 1)
                    nc.vector.tensor_reduce(f_ss[:, :], f_in[:, :].rearrange("p (n d) -> p n d", d=FD), AX.X, ALU.add
                                            ).then_inc(o_ss, 1)
                    dve.wait_ge(o_r, i + 1)
                    tt_(o16, o16, bc(f_r[:, :], FD), ALU.mult).then_inc(o_scaled, 1)
                    dve.wait_ge(o_scaled, i + 1)
                    tt_(o16, o16, vec[:, V_FO:V_FO + FD].unsqueeze(1).to_broadcast([P, NT * 2, FD]), ALU.mult
                        ).then_inc(o_normed, 1)

                def four(ap):
                    return ap.rearrange("p (c n) -> p c n", c=4)

                def per_chunk(kind, h):
                    return bc(g_sc[:, kind, 4 * h:4 * h + 4], P)

                def normed(h, n):
                    dve.wait_ge(g_rd[h], n)
                    tt_(four(n_tok[h]), four(ps[:, 6 + h, :]), bc(g_r[:, h, :], P), ALU.mult).then_inc(g_empty[6 + h], 1)

                def k_in(h):
                    dve.wait_ge(g_sqd[h], i * 2 + 1)
                    nc.vector.tensor_reduce(g_ss[:, h, :], four(n_tok[h]), AX.X, ALU.add).then_inc(g_ssd[h], 1)
                    tt_(four(decay[h]), tri.unsqueeze(1).to_broadcast([P, 4, P]), per_chunk(K_G, h), ALU.mult
                        ).then_inc(g_tri[h], 1)
                    normed(h, i * 2 + 1)
                    dve.wait_ge(g_empty[6 + h], empty(i, ("k_in", h), 6 + h))
                    tt_(four(kb_tok[h]), four(n_tok[h]), per_chunk(K_BETA, h), ALU.mult).then_inc(g_tok[h], 1)
                    tt_(four(kd[h]), four(n_tok[h]), per_chunk(K_EKD, h), ALU.mult).then_inc(g_tok[h], 1)

                def kb_t(h):
                    dve.wait_ge(g_full[6 + h], full(i, ("kb_t", h), 6 + h))
                    tt_(four(kb_tok[h]), four(kb_tok[h]), per_chunk(K_EG, h), ALU.mult).then_inc(g_tok[h], 1)

                def q_in(h):
                    dve.wait_ge(g_sqd[h], i * 2 + 2)
                    nc.vector.tensor_reduce(g_ss[:, h, :], four(qe_tok[h]), AX.X, ALU.add).then_inc(g_ssd[h], 1)
                    normed(h, i * 2 + 2)
                    dve.wait_ge(g_empty[6 + h], empty(i, ("q_in", h), 6 + h))
                    tt_(four(qe_tok[h]), four(n_tok[h]), per_chunk(K_EG, h), ALU.mult).then_inc(g_tok[h], 1)

                def v_in(h):
                    b = 6 + h
                    dve.wait_ge(g_full[b], full(i, ("v_in", h), b))
                    tt_(four(vb[h]), four(ps[:, b, :]), per_chunk(K_BETA, h), ALU.mult).then_inc(g_empty[b], 1)

                def kk(h):
                    b = 6 + h
                    dve.wait_ge(g_full[b], full(i, ("kk", h), b))
                    tt_(kbT[h], ps[:, b, :], decay[h], ALU.mult).then_inc(g_empty[b], 1)
                    dve.wait_ge(g_empty[b], empty(i, ("kk", h), b))
                    tt_(tmT[h], lt[h], cst[:, C_M0:C_M0 + P].unsqueeze(1).to_broadcast([P, 4, P]), ALU.mult
                        ).then_inc(t_init[h], 1)
                    dve.wait_ge(t_init[h], i * 2 + 1)
                    tt_(tmT[h], tmT[h], ident.unsqueeze(1).to_broadcast([P, 4, P]), ALU.add).then_inc(t_init[h], 1)

                def kq(h):
                    b = 6 + h
                    dve.wait_ge(g_full[b], full(i, ("kq", h), b))
                    tt_(intra[h], ps[:, b, :], decay[h], ALU.mult).then_inc(g_empty[b], 1)

                def lt_(h, l):
                    b = 6 + h
                    dve.wait_ge(g_full[b], full(i, ("lt", h, l), b))
                    c0 = C_LV + (l - 1) * (P // 2)
                    tt_(lt_t[h], ps[:, b, 0:4 * (P // 2)].rearrange("p (c n) -> p c n", c=4),
                        cst[:, c0:c0 + P // 2].unsqueeze(1).to_broadcast([P, 4, P // 2]), ALU.mult).then_inc(g_empty[b], 1)

                def tlt(h, l):
                    b = 6 + h
                    dve.wait_ge(g_full[b], full(i, ("tlt", h, l), b))
                    first = evens(tm[h], l)
                    tt_(first, first, blocks(ps[:, b, 0:4 * (P // 2)].rearrange("p (c n) -> p c n", c=4), l),
                        ALU.subtract).then_inc(g_empty[b], 1)

                def u_(h):
                    b = 6 + h
                    dve.wait_ge(g_full[b], full(i, ("u", h), b))
                    nc.vector.tensor_copy(qT[h], ps[:, b, :]).then_inc(g_empty[b], 1)

                def read(h, c):
                    dve.wait_ge(g_full[6], full(i, ("read", h, c), 6))
                    if c == 0:
                        dve.wait_ge(g_empty[6 + h], empty(i, ("u", h), 6 + h))
                    tt_(vnew[:, :], u_tok[h][:, c, :], ps[:, 6, 0:P], ALU.subtract).then_inc(g_empty[6], 1)

                def write(h, c):
                    dve.wait_ge(g_full[6], full(i, ("write", h, c), 6))
                    n = 4 * h + c
                    stt(state[:, :], state[:, :], g_sc[:, K_EGL, n:n + 1], ps[:, 6, 0:P], ALU.mult, ALU.add
                        ).then_inc(g_empty[6], 1)

                def gdn_norm():
                    dve.wait_ge(gn_rms, i + 1)
                    stt(gv, gv, vec[:, V_GON:V_GON + 1], gq, ALU.mult, ALU.mult).then_inc(gn_scaled, 1)
                    dve.wait_ge(gn_scaled, i + 1)
                    tt_(gz, gz, gv, ALU.mult).then_inc(g_out, 1)

                nc.vector.tensor_copy(conv_taps[:, :, :], conv_all[:, :, bass.ds(i, 1), :].rearrange("p t a j -> p t (a j)")
                                      ).then_inc(head_ready, 1)
                dve.wait_ge(head_ready, i * 3 + 3)

                step = {"proj": proj, "silu": silu, "fox_in": fox_in, "scores": scores, "turn": turn, "values": values,
                        "fox_norm": fox_norm, "k_in": k_in, "kb_t": kb_t, "q_in": q_in, "v_in": v_in, "kk": kk, "kq": kq,
                        "lt": lt_, "tlt": tlt, "u": u_, "read": read, "write": write, "gdn_norm": gdn_norm}
                for name, *args in SCHEDULE:
                    if name in step:
                        step[name](*args)
            tail_vector(dve)


_NAMES = ["xt", "memt", "wstream", "wgate", "consts", "vecs"]


def _consts(np):
    r, c = np.arange(P)[:, None], np.arange(P)[None, :]
    parts = [r == c, r <= c, np.ones((P, P)), -1.0 * ((c == r + 1) & (r % 2 == 0)),
             np.where(c > r, NEG, 0.0), np.where(c < r, NEG, 0.0)]
    for l in range(1, LEVELS):
        s = 2 ** l
        col = np.arange(P // 2)
        col = col // s * 2 * s + col % s
        parts.append(r // s == col[None, :] // s + 1)
    return np.concatenate([np.asarray(p, np.float32) for p in parts], axis=1)


def _tiles(np, w):
    k, m = w.shape
    return w.reshape(k // P, P, m // P, P).transpose(2, 1, 0, 3).reshape(m // P, P, -1)


def _columns(np, v):
    return v.reshape(-1, P).T


def kernel(**inputs):
    import numpy as np
    import concourse.bacc as bacc
    from concourse.bass_utils import run_bass_kernel_spmd as run

    a = {k: np.asarray(v) for k, v in inputs.items()}
    w_in = a["w_in"][0]
    fox, gate_f, gdn, gate_ba, z = np.split(
        w_in, np.cumsum([3 * FH * FD, FH, 3 * GH * GD, 2 * GH]).tolist(), axis=1)
    fox_t, gdn_t, z_t = _tiles(np, fox), _tiles(np, gdn), _tiles(np, z)
    stream = []
    for i in range(STEPS):
        stream += [gdn_t[GH + i], gdn_t[i], gdn_t[2 * GH + i], fox_t[i], fox_t[STEPS + i], fox_t[2 * STEPS + i], z_t[i]]
    stream += list(_tiles(np, a["w_out"][0])) + list(_tiles(np, a["w_ckv"][0])) + list(_tiles(np, a["w_cq"][0]))

    def pairs(w):
        t = _tiles(np, w)
        return list(t.reshape(t.shape[0] // 2, 2, P, -1).transpose(0, 2, 1, 3).reshape(t.shape[0] // 2, P, -1))

    stream += pairs(a["w_co"][0])
    w1 = _tiles(np, a["w_mlp1"][0])
    w2 = a["w_mlp2"][0]
    for g in range(FF_GROUPS):
        stream += list(w1[FF_PER * g:FF_PER * (g + 1)]) + pairs(w2[FF_PER * P * g:FF_PER * P * (g + 1)])
    conv = a["gdn_conv_w"][0].reshape(CONV, 3 * GH, P).transpose(2, 1, 0).reshape(P, -1)
    bias = np.concatenate([a["fox_f_bias"][0], np.zeros(GH, np.float32), a["gdn_dt_bias"][0]])
    every = lambda v: np.broadcast_to(v[None, :], (P, v.shape[0]))
    vecs = np.concatenate([_columns(np, a[n][0]) for n in ("norm_mix_g", "norm_xattn_g", "mem_norm_g", "norm_mlp_g")]
                          + [conv] + [_columns(np, a[n][0]) for n in ("gdn_onorm_g", "xattn_qnorm_g", "xattn_knorm_g")]
                          + [every(bias), every(a["gdn_A_log"][0]), every(a["fox_qnorm_g"][0]),
                             every(a["fox_knorm_g"][0]), every(a["fox_onorm_g"][0])], axis=1)
    arrays = {
        "xt": a["x"][0].T.reshape(KT, P, S),
        "memt": a["mem"][0].T.reshape(KT, P, MEM).transpose(1, 0, 2),
        "wstream": np.stack(stream),
        "wgate": np.concatenate([gate_f, gate_ba], axis=1).reshape(KT, P, GATES).transpose(1, 0, 2),
        "consts": _consts(np),
        "vecs": vecs,
    }
    arrays = {k: np.ascontiguousarray(v) for k, v in arrays.items()}
    nc = bacc.Bacc("TRN2", target_bir_lowering=False, num_devices=1)
    args = [nc.dram_tensor(n, arrays[n].shape, F32, kind="ExternalInput").ap() for n in _NAMES]
    out = nc.dram_tensor("out", (KT, P, S), F32, kind="ExternalOutput").ap()
    build_layer(nc, *args, out)
    r = run(nc, [arrays], core_ids=[0])
    return np.ascontiguousarray(r.results[0]["out"].reshape(D, S).T)[None]
```
